# Optimizing a Trainium2 kernel written in Bass

```python
import jax, jax.numpy as jnp
from jax import lax
import numpy as np

D_MODEL = 1024
BATCH = 1
SEQ = 1024
DEPTH = 2
DEC_BATCH = 1
DEC_SEQ = 64
PAST_LEN = 128

CHUNK = 64
D_CONV = D_MODEL
CONV_W = 3
RET_HEADS = 4
RET_DK = D_MODEL // 8
RET_DV = D_MODEL // 4
D_QK = RET_HEADS * RET_DK
D_RV = RET_HEADS * RET_DV
IN_SIZES = (D_CONV, D_CONV, D_CONV, D_CONV, D_QK, D_QK, D_RV, D_RV, D_MODEL, D_MODEL)
D_IN = sum(IN_SIZES)
ROPE_BASE = 10000.0
EPS = 1e-6

kernel_name = "gated_shortconv_retention_stream_step"

def rmsnorm(x, g):
    xf = x.astype(jnp.float32)
    y = xf * lax.rsqrt(jnp.mean(xf * xf, axis=-1, keepdims=True) + EPS)
    return (y * g.astype(jnp.float32)).astype(x.dtype)

def head_norm(o):
    return o * lax.rsqrt(jnp.mean(o * o, axis=-1, keepdims=True) + EPS)

def rotary(x, pos):
    half = RET_DK // 2
    inv = 1.0 / (ROPE_BASE ** (jnp.arange(half, dtype=jnp.float32) / half))
    ang = pos.astype(jnp.float32)[:, None] * inv[None, :]
    cos = jnp.cos(ang)[None, :, None, :]
    sin = jnp.sin(ang)[None, :, None, :]
    xf = x.astype(jnp.float32)
    x1, x2 = xf[..., :half], xf[..., half:]
    return jnp.concatenate([x1 * cos - x2 * sin, x1 * sin + x2 * cos], axis=-1)

def retention_chunk(q, k, v, s_prev, log_gamma):
    L = q.shape[2]
    idx = jnp.arange(L, dtype=jnp.float32)
    rel = idx[:, None] - idx[None, :]
    lg = log_gamma[:, None, None]
    decay = jnp.where(rel >= 0, jnp.exp(lg * jnp.maximum(rel, 0.0)), 0.0)
    scores = jnp.einsum('bhid,bhjd->bhij', q, k) * decay[None]
    o = jnp.einsum('bhij,bhjv->bhiv', scores, v)
    q_dec = jnp.exp(log_gamma[:, None] * (idx + 1.0))[None, :, :, None]
    o = o + jnp.einsum('bhid,bhdv->bhiv', q, s_prev) * q_dec
    k_dec = jnp.exp(log_gamma[:, None] * (L - 1.0 - idx))[None, :, :, None]
    s_new = (jnp.exp(log_gamma * L)[None, :, None, None] * s_prev
             + jnp.einsum('bhjd,bhjv->bhdv', k * k_dec, v))
    return o, s_new

def retention(q, k, v, s_prev, log_gamma):
    Bn, T = q.shape[0], q.shape[1]
    q, k, v = (a.transpose(0, 2, 1, 3) for a in (q, k, v))
    if T <= CHUNK:
        o, s = retention_chunk(q, k, v, s_prev, log_gamma)
    else:
        n = T // CHUNK

        def to_chunks(a):
            return a.reshape(Bn, RET_HEADS, n, CHUNK, a.shape[-1]).transpose(2, 0, 1, 3, 4)

        def body(s, qkv):
            qc, kc, vc = qkv
            oc, s_next = retention_chunk(qc, kc, vc, s, log_gamma)
            return s_next, oc

        s, oc = lax.scan(body, s_prev, (to_chunks(q), to_chunks(k), to_chunks(v)))
        o = oc.transpose(1, 2, 0, 3, 4).reshape(Bn, RET_HEADS, T, RET_DV)
    return o.transpose(0, 2, 1, 3), s

def mixer_layer(x, conv_buf, s_prev, pos, g, w_in, conv_w, w_a, w_r, w_o, log_gamma):
    Bn, T, _ = x.shape
    h = rmsnorm(x, g)
    p = h @ w_in
    split_at = np.cumsum(IN_SIZES)[:-1].tolist()
    hc, b, c, z_a, q, k, v, z_r, g_a, g_r = jnp.split(p, split_at, axis=-1)
    u = c * hc
    u_pad = jnp.concatenate([conv_buf.astype(u.dtype), u], axis=1)
    conv = (conv_w[0] * u_pad[:, 0:T] + conv_w[1] * u_pad[:, 1:T + 1]
            + conv_w[2] * u_pad[:, 2:T + 2])
    a = ((b * conv) * jax.nn.silu(z_a)) @ w_a
    new_buf = u_pad[:, -(CONV_W - 1):]
    qr = rotary(q.reshape(Bn, T, RET_HEADS, RET_DK), pos)
    kr = rotary(k.reshape(Bn, T, RET_HEADS, RET_DK), pos) * (RET_DK ** -0.5)
    vr = v.reshape(Bn, T, RET_HEADS, RET_DV).astype(jnp.float32)
    o, s_new = retention(qr, kr, vr, s_prev.astype(jnp.float32), log_gamma)
    o = head_norm(o).astype(x.dtype).reshape(Bn, T, D_RV)
    r = (o * jax.nn.silu(z_r)) @ w_r
    merged = jax.nn.sigmoid(g_a) * a + jax.nn.sigmoid(g_r) * r
    return x + merged @ w_o, new_buf, s_new

def setup_inputs(seed: int = 0) -> dict:
    key = jax.random.key(seed)
    ks = jax.random.split(key, 12)
    f32 = jnp.float32
    x_prompt = jax.random.normal(ks[0], (BATCH, SEQ, D_MODEL), f32)
    x_sample = jax.random.normal(ks[1], (DEC_BATCH, DEC_SEQ, D_MODEL), f32)
    state_conv = jax.random.normal(ks[2], (DEPTH, DEC_BATCH, CONV_W - 1, D_CONV), f32)
    state_ret = 0.5 * jax.random.normal(ks[3], (DEPTH, DEC_BATCH, RET_HEADS, RET_DK, RET_DV), f32)
    norm_g = 1.0 + 0.02 * jax.random.normal(ks[4], (DEPTH, D_MODEL), f32)
    w_in = jax.random.normal(ks[5], (DEPTH, D_MODEL, D_IN), f32) * D_MODEL ** -0.5
    conv_w = jax.random.normal(ks[6], (DEPTH, CONV_W, D_CONV), f32) * CONV_W ** -0.5
    w_a = jax.random.normal(ks[7], (DEPTH, D_CONV, D_MODEL), f32) * D_CONV ** -0.5
    w_r = jax.random.normal(ks[8], (DEPTH, D_RV, D_MODEL), f32) * D_RV ** -0.5
    w_o = jax.random.normal(ks[9], (DEPTH, D_MODEL, D_MODEL), f32) * D_MODEL ** -0.5
    final_g = 1.0 + 0.02 * jax.random.normal(ks[10], (D_MODEL,), f32)
    return {"x_prompt": x_prompt, "x_sample": x_sample, "state_conv": state_conv,
            "state_ret": state_ret, "norm_g": norm_g, "w_in": w_in, "conv_w": conv_w,
            "w_a": w_a, "w_r": w_r, "w_o": w_o, "final_g": final_g}

def reference(x_prompt, x_sample, state_conv, state_ret, norm_g, w_in, conv_w, w_a, w_r, w_o, final_g):
    log_gamma = jnp.log(1.0 - 2.0 ** (-5.0 - jnp.arange(RET_HEADS, dtype=jnp.float32)))
    Bp, Tp = x_prompt.shape[0], x_prompt.shape[1]
    Ts = x_sample.shape[1]
    pos_p = jnp.arange(Tp, dtype=jnp.int32)
    pos_s = PAST_LEN + jnp.arange(Ts, dtype=jnp.int32)
    buf_p0 = jnp.zeros((Bp, CONV_W - 1, D_CONV), x_prompt.dtype)
    s_p0 = jnp.zeros((Bp, RET_HEADS, RET_DK, RET_DV), jnp.float32)
    xp, xs = x_prompt, x_sample
    conv_p, ret_p, conv_s, ret_s = [], [], [], []
    for l in range(DEPTH):
        xp, bp, sp = mixer_layer(xp, buf_p0, s_p0, pos_p, norm_g[l], w_in[l], conv_w[l],
                                 w_a[l], w_r[l], w_o[l], log_gamma)
        xs, bs, ss = mixer_layer(xs, state_conv[l], state_ret[l], pos_s, norm_g[l], w_in[l],
                                 conv_w[l], w_a[l], w_r[l], w_o[l], log_gamma)
        conv_p.append(bp)
        ret_p.append(sp)
        conv_s.append(bs)
        ret_s.append(ss)
    y_prompt = rmsnorm(xp, final_g)
    y_sample = rmsnorm(xs, final_g)
    return (y_prompt, y_sample, jnp.stack(conv_p), jnp.stack(ret_p), jnp.stack(conv_s), jnp.stack(ret_s))


_drawn_inputs = setup_inputs


def setup_inputs(seed=0):
    import zlib

    import numpy as np

    out = dict(_drawn_inputs(seed))
    spreads = {}
    factors = {}
    for name, (base, spread) in spreads.items():
        noise = np.random.default_rng([zlib.crc32(name.encode()), seed]).standard_normal(out[name].shape)
        drawn = base * np.exp(spread * noise) if base else spread * noise
        out[name] = __import__('jax').numpy.asarray(drawn.astype(out[name].dtype))
    for name, factor in factors.items():
        out[name] = (out[name] * factor).astype(out[name].dtype)
    return out
```

```python
import concourse.bass as bass
from concourse import mybir
from contextlib import ExitStack

F32 = mybir.dt.float32
F32R = mybir.dt.float32r
ALU = mybir.AluOpType
ACT = mybir.ActivationFunctionType
ds = bass.ds

P = 128
D = 1024
KT = D // P
SEQ, DEC, PAST = 1024, 64, 128
LAYERS = 2
HEADS, DK, DV = 4, 128, 256
CHUNK = 128
NCH = SEQ // CHUNK
GAP = SEQ
SAMP = SEQ + 2
TAIL = SAMP + DEC
COLS = TAIL + 2
BANK = 512
THIRD = COLS // 3
EPS = 1e-6
OPEN = 1

HC, B_, C_, ZA, Q_, K_, V_, ZR, GA, GR = 0, 1024, 2048, 3072, 4096, 4608, 5120, 6144, 7168, 8192

WL = 96
UL = 120
BL = 52
W_GR, W_A, W_AG, W_O = 32, 40, 72, 88
U_GR, U_A, U_AG, U_O = 56, 64, 96, 112

MASK, KDEC, KDECS, OA_, OB_, G128, G64 = 0, 128, 129, 130, 131, 132, 133
NHC = 134
PG, PW, PF, PS = 0, 16, 64, 72
NPAR = 104


def build(nc, x_prompt, x_sample, state_conv, state_ret, norm_g, w_in, conv_w, w_a, w_r, w_o, final_g,
          rope_c, head_c, ident_c, y_prompt, y_sample, conv_p, ret_p, conv_s, ret_s, x_keep):
    with ExitStack() as ctx:
        base = (nc.sbuf_base + 63) // 64 * 64
        size = 212 * 1024 - 5 * 1024
        at = [0]

        def place(name, shape, dtype, offset=None):
            n = 4
            for s in shape[1:]:
                n *= s
            if dtype == mybir.dt.bfloat16:
                n //= 2
            if offset is None:
                offset = at[0]
                at[0] += (n + 31) // 32 * 32
            return nc.alloc_sbuf_tensor_at(name, shape, dtype, offset=base + offset), (offset + n + 31) // 32 * 32

        TILE = COLS * 4
        act_hi, _ = place("act_hi", [P, KT, COLS], F32R)
        act_lo, _ = place("act_lo", [P, KT, COLS], F32R)
        y_rows, _ = place("y_rows", [P, NCH + 1, D], F32, offset=0)
        row_squares, _ = place("row_squares", [P, NCH + 1, D], mybir.dt.bfloat16, offset=0)
        r_at = at[0]
        r, _ = place("r", [P, KT, COLS], F32)
        x_rows, _ = place("x_rows", [P, NCH, D], F32, offset=r_at)
        area = at[0]
        at[0] += 2 * KT * TILE
        x, _ = place("x", [P, KT, COLS], F32, offset=area)
        prod_hi, e = place("prod_hi", [P, KT, COLS], F32R, offset=area)
        prod_lo, _ = place("prod_lo", [P, KT, COLS], F32R, offset=e)
        rstd_row, _ = place("rstd_row", [P, COLS], F32, offset=area + KT * TILE)
        g_rows, _ = place("g_rows", [P, D], F32, offset=area + KT * TILE)
        o_hi, e = place("o_hi", [P, 2, COLS], F32R, offset=area)
        o_lo, e = place("o_lo", [P, 2, COLS], F32R, offset=e)
        qT, e = place("qT", [P, COLS], F32, offset=e)
        kT, _ = place("kT", [P, COLS], F32, offset=e)
        S, e = place("S", [P, NCH + 2, DV], F32, offset=e)
        V, e = place("V", [P, NCH + 1, DV], F32, offset=e)
        K, e = place("K", [P, NCH + 1, DK], F32, offset=e)
        Pr, e = place("Pr", [P, NCH + 1, CHUNK], F32, offset=e)
        zs, e = place("zs", [P, 2, COLS], F32, offset=e)
        rope, e = place("rope", [P, 2, COLS], F32, offset=e)
        junk = []
        for c in range(4):
            t, e2 = place(f"junk{c}", [P, DV], mybir.dt.bfloat16, offset=e if c < 3 else None)
            junk.append(t)
            e = e2 if c < 3 else e
        assert e <= area + 2 * KT * TILE
        w_raw = [place(f"w_raw{s}", [P, D], F32)[0] for s in range(2)]
        w_hi = [place(f"w_hi{s}", [P, D], F32R)[0] for s in range(2)]
        w_lo = [place(f"w_lo{s}", [P, D], F32R)[0] for s in range(2)]
        T0, _ = place("T0", [P, COLS], F32)
        t1_at = at[0]
        U, _ = place("U", [P, COLS + 4], F32)
        par_rows, _ = place("par_rows", [P, P], F32, offset=t1_at + 64)
        T1 = U[:, 2:2 + COLS]
        ident, _ = place("ident", [P, P + 2], F32)
        ones, _ = place("ones", [P, P], F32)
        par, _ = place("par", [P, NPAR], F32)
        hc, _ = place("hc", [P, NHC], F32)
        conv_keep, _ = place("conv_keep", [P, 2, 2, KT], F32)
        sums, _ = place("sums", [P, 9], F32)
        means, _ = place("means", [P, 9], F32)
        power, _ = place("power", [P, 9], F32)
        rstds, _ = place("rstds", [P, 9], F32)
        neg_half, _ = place("neg_half", [P, 9], F32)
        zero, _ = place("zero", [P, 1], F32)
        assert at[0] <= nc.sbuf_usable_end - base, (at[0], nc.sbuf_usable_end - base)
        I = ident[:, 2:2 + P]

        ps = ctx.enter_context(nc.psum_tensor("ps", [P, 8, BANK], F32))
        psf = ps[:, :, :].rearrange("p b n -> p (b n)")

        def slot(s):
            return ps[:, 3 * s:3 * s + 3, 0:THIRD]

        def cols(a):
            return a.rearrange("p (c n) -> p c n", c=3)

        small = psf[:, 6 * BANK:8 * BANK]
        small_k = small.rearrange("p (c n) -> p c n", n=CHUNK)
        small_v = small.rearrange("p (c n) -> p c n", n=DV)
        k_s = ps[0:DEC, 6, 0:DK]
        v_s = ps[0:DEC, 6, DK:DK + DV]
        score_s = ps[0:DEC, 7, 0:DEC]
        o_s = ps[:, 6, 0:2 * DEC].rearrange("p (v n) -> p v n", v=2)
        T1s = T1[:, 0:2 * DEC].rearrange("p (v n) -> p v n", v=2)

        def sem(name):
            return ctx.enter_context(nc.semaphore(name))

        ident_loaded = sem("ident_loaded")
        consts_loaded = sem("consts_loaded")
        ones_set = sem("ones_set")
        rows_loaded = [sem(f"rows_loaded{c}") for c in range(NCH + 1)]
        gaps_set = sem("gaps_set")
        params_turned = sem("params_turned")
        params_ready = sem("params_ready")
        rows_turned = sem("rows_turned")
        rows_squared = sem("rows_squared")
        u_cleared = sem("u_cleared")
        x_cols_act = sem("x_cols_act")
        x_cols_dve = sem("x_cols_dve")
        weights_loaded = [sem(f"weights_loaded{s}") for s in range(2)]
        weights_hi = sem("weights_hi")
        weights_split = sem("weights_split")
        weights_started = sem("weights_started")
        unit_done = sem("unit_done")
        slot_read = [sem(f"slot_read{s}") for s in range(2)]
        small_done = sem("small_done")
        small_read = sem("small_read")
        ssq_cleared = sem("ssq_cleared")
        squared = sem("squared")
        ssq_added = sem("ssq_added")
        norm_summed = sem("norm_summed")
        mean_ready = sem("mean_ready")
        norm_power = sem("norm_power")
        diag_ready = sem("diag_ready")
        rstd_spread = sem("rstd_spread")
        rstd_copied = sem("rstd_copied")
        normed = sem("normed")
        h_hi_ready = sem("h_hi_ready")
        h_ready = sem("h_ready")
        x_stored = sem("x_stored")
        x_loaded = [sem(f"x_loaded{g}") for g in range(4)]
        rope_loaded = sem("rope_loaded")
        head_loaded = sem("head_loaded")
        state_loaded = sem("state_loaded")
        states_stored = sem("states_stored")
        swapped = sem("swapped")
        swapped_sin = sem("swapped_sin")
        roped = sem("roped")
        z_gate = sem("z_gate")
        scanned = sem("scanned")
        sample_state = sem("sample_state")
        o_squared = sem("o_squared")
        o_mean = sem("o_mean")
        o_power = sem("o_power")
        o_rstd = sem("o_rstd")
        sample_copied = sem("sample_copied")
        o_hi_ready = sem("o_hi_ready")
        o_split = sem("o_split")
        r_cleared = sem("r_cleared")
        r_gated = sem("r_gated")
        conv_kept = sem("conv_kept")
        conv_stored = sem("conv_stored")
        u_ready = sem("u_ready")
        conv_first = sem("conv_first")
        conv_second = sem("conv_second")
        conv_third = sem("conv_third")
        a_gate = sem("a_gate")
        a_product = sem("a_product")
        a_hi_ready = sem("a_hi_ready")
        a_split = sem("a_split")
        merged = sem("merged")
        m_hi_ready = sem("m_hi_ready")
        m_split = sem("m_split")
        y_turned = sem("y_turned")
        y_read = sem("y_read")
        y_stored = sem("y_stored")
        g_loaded = sem("g_loaded")

        block = ctx.enter_context(nc.Block())

        def chunk_cols(c):
            return (c * CHUNK, CHUNK) if c < NCH else (SAMP, DEC)

        def head_bases(l, h):
            if isinstance(h, int) and h == 0:
                return l * WL, l * (UL // 2), l * BL
            return l * WL + h * 8 - 2, l * (UL // 2) + h * 7 - 4, l * BL + h * 13 - 3

        B_KT, B_SC, B_V0, B_V1, B_X, B_KVA, B_KVB, B_S, B_OA, B_OB = range(10)

        @block.sync
        def _(sp):
            sp.sem_inc(conv_stored, OPEN)
            sp.dma_start(ident[:, :], ident_c).then_inc(ident_loaded, 16)
            for c in range(NCH):
                sp.dma_start(x_rows[:, c, :], x_prompt[0, c * P:(c + 1) * P, :]).then_inc(rows_loaded[c], 16)
            sp.dma_start(T0[0:DEC, 0:D], x_sample[0]).then_inc(rows_loaded[NCH], 16)

            def load(n, s, src, shape_k, first=False):
                if not first:
                    sp.wait_ge(weights_split, n - 1)
                sp.dma_start(w_raw[s][:, :].rearrange("p (k n) -> p k n", k=shape_k), src).then_inc(weights_loaded[s], 16)

            def w_in_at(l, col):
                return w_in[l, :, ds(col, P)].rearrange("(k p) n -> p k n", p=P)

            def w_r_at(l, h, half):
                return w_r[l, ds(h * DV, DV), half * 512:half * 512 + 512].rearrange("(k p) n -> p k n", p=P)

            def loads_head(l, h, j0=0):
                wb, _, _ = head_bases(l, h)
                order = [K_ + h * DK, Q_ + h * DK, V_ + h * DV, V_ + h * DV + P, ZR + h * DV, ZR + h * DV + P]
                first = isinstance(h, int)
                if not first:
                    order[2:2] = [None, None]
                for j, col in enumerate(order):
                    if j < j0:
                        continue
                    load(wb + j, j % 2, w_r_at(l, h - 1, j - 2) if col is None else w_in_at(l, col), 2 if col is None else KT)

            for j, col in enumerate((K_, Q_)):
                load(j, j, w_in_at(0, col), KT, first=True)
            for l in range(LAYERS):
                if l == 0:
                    sp.wait_ge(x_cols_act, 5)
                    sp.wait_ge(x_cols_dve, 4)
                    for g in range(4):
                        sp.dma_start(x_keep[:, 2 * g:2 * g + 2, :], x[:, 2 * g:2 * g + 2, :]).then_inc(x_stored, 16)
                sp.wait_ge(x_stored, 64 * (l + 1))
                sp.wait_ge(h_ready, KT * (l + 1))
                sp.dma_start(rope[:, :, :], rope_c.rearrange("a p n -> p a n")).then_inc(rope_loaded, 16)
                loads_head(l, 0, j0=2)
                with sp.Fori(1, HEADS) as h:
                    loads_head(l, h)
                for j in range(2):
                    load(l * WL + W_GR - 2 + j, j, w_in_at(l, GR + j * P), KT)
                for half in range(2):
                    load(l * WL + W_GR + half, half, w_r_at(l, HEADS - 1, half), 2)
                with sp.Fori(1, KT // 2) as i:
                    for j in range(2):
                        load(l * WL + W_GR + i * 2 + j, j, w_in_at(l, GR + i * (2 * P) + j * P), KT)
                with sp.Fori(0, KT) as m:
                    for j, part in enumerate((HC, C_, B_, ZA)):
                        load(l * WL + W_A + m * 4 + j, j % 2, w_in_at(l, part + m * P), KT)
                with sp.Fori(0, KT) as m:
                    sp.wait_ge(weights_split, l * WL + W_AG + m * 2)
                    load(0, 0, w_in_at(l, GA + m * P), KT, first=True)
                    load(0, 1, w_a[l, :, ds(m * P, P)].rearrange("(k p) n -> p k n", p=P), KT, first=True)
                for j in range(2):
                    load(l * WL + W_O + j, j, w_o[l, :, j * P:(j + 1) * P].rearrange("(k p) n -> p k n", p=P), KT)
                sp.wait_ge(unit_done, l * UL + U_O + OPEN)
                for g in range(4):
                    sp.dma_start(x[:, 2 * g:2 * g + 2, :], x_keep[:, 2 * g:2 * g + 2, :]).then_inc(x_loaded[g], 16)
                if l == LAYERS - 1:
                    sp.dma_start(g_rows[:, :], final_g.rearrange("(a n) -> a n", a=1).to_broadcast([P, D])).then_inc(g_loaded, 16)
                sp.wait_ge(conv_kept, KT * (l + 1))
                with nc.allow_non_contiguous_dma(reason="two rows of 1024 from feature-major columns"):
                    for row in range(2):
                        sp.dma_start(conv_p[l, 0, row].rearrange("(k p) -> p k", p=P), conv_keep[:, 0, row, :]).then_inc(conv_stored, 16)
                        sp.dma_start(conv_s[l, 0, row].rearrange("(k p) -> p k", p=P), conv_keep[:, 1, row, :]).then_inc(conv_stored, 16)
                with sp.Fori(1, KT // 2) as i:
                    for j in range(2):
                        load(l * WL + W_O + i * 2 + j, j, w_o[l, :, ds(i * (2 * P) + j * P, P)].rearrange("(k p) n -> p k n", p=P), KT)
                if l < LAYERS - 1:
                    for j, col in enumerate((K_, Q_)):
                        load((l + 1) * WL + j, j, w_in_at(l + 1, col), KT)
                    for g in range(4):
                        sp.wait_ge(slot_read[0], l * (UL // 2) + U_O // 2 + g + 1 + OPEN)
                        sp.wait_ge(slot_read[1], l * (UL // 2) + U_O // 2 + g + 1 + OPEN)
                        sp.dma_start(x_keep[:, 2 * g:2 * g + 2, :], x[:, 2 * g:2 * g + 2, :]).then_inc(x_stored, 16)
            for c in range(NCH + 1):
                sp.wait_ge(y_read, c + 1)
                if c < NCH:
                    sp.dma_start(y_prompt[0, c * P:(c + 1) * P, :], y_rows[:, c, :]).then_inc(y_stored, 16)
                else:
                    sp.dma_start(y_sample[0], y_rows[0:DEC, c, :]).then_inc(y_stored, 16)
            sp.wait_ge(y_stored, 16 * (NCH + 1))
            sp.wait_ge(conv_stored, 64 * LAYERS + OPEN)
            sp.wait_ge(states_stored, 32 * HEADS * LAYERS + OPEN)

        @block.gpsimd
        def _(pool):
            nc.gpsimd.memset(ones[:, :], 1.0).then_inc(ones_set, 1)
            nc.gpsimd.memset(neg_half[:, :], -0.5).then_inc(ones_set, 1)
            nc.gpsimd.memset(zero[:, :], 0.0).then_inc(ones_set, 1)
            pool.wait_ge(ones_set, 3)

            def split(n, n2, s, units_before=None):
                pool.wait_ge(weights_loaded[s], n2 * 16 + 16)
                if units_before is None:
                    pool.wait_ge(weights_started, n + OPEN)
                else:
                    pool.wait_ge(unit_done, units_before + OPEN)
                nc.gpsimd.tensor_tensor(w_hi[s][:, :], w_raw[s][:, :], zero[:, 0:1].to_broadcast([P, D]), ALU.add).then_inc(weights_hi, 1)
                pool.wait_ge(weights_hi, n + 1)
                nc.gpsimd.tensor_tensor(w_lo[s][:, :], w_raw[s][:, :], w_hi[s][:, :].bitcast(F32),
                                        ALU.subtract).then_inc(weights_split, 1)

            def norm_rstd(k):
                pool.wait_ge(mean_ready, k + 1)
                nc.gpsimd.tensor_tensor(power[:, :], means[:, :], neg_half[:, :], ALU.pow).then_inc(norm_power, 1)

            def o_pow(i, rows, c0, n):
                pool.wait_ge(o_mean, i + 1)
                nc.gpsimd.tensor_tensor(power[0:rows, c0:c0 + n], means[0:rows, c0:c0 + n],
                                        neg_half[0:rows, c0:c0 + n], ALU.pow).then_inc(o_power, 1)

            def head(l, h):
                wb, _, _ = head_bases(l, h)
                w2 = l * (WL // 2) + (0 if isinstance(h, int) else h * 4 - 1)
                first = isinstance(h, int)
                n3 = (l * HEADS + h) * 3
                for j in range(2 if first else 1, 6 if first else 8):
                    split(wb + j, w2 + j // 2, j % 2)
                last = 6 if first else 8
                split(wb + last, w2 + last // 2, 0)
                o_pow(n3, DEC, 8, 1)
                o_pow(n3 + 1, P, 0, 4)
                o_pow(n3 + 2, P, 4, 4)

            with pool.Fori(0, LAYERS) as l:
                split(l * WL, l * (WL // 2), 0)
                norm_rstd(l)
                split(l * WL + 1, l * (WL // 2), 1, l * UL)
                head(l, 0)
                with pool.Fori(1, HEADS) as h:
                    head(l, h)
                split(l * WL + W_GR - 1, l * (WL // 2) + W_GR // 2 - 1, 1)
                with pool.Fori(W_GR // 2, WL // 2) as i:
                    for j in range(2):
                        split(l * WL + i * 2 + j, l * (WL // 2) + i, j)
            norm_rstd(LAYERS)

        @block.scalar
        def _(act):
            act.sem_inc(states_stored, OPEN)
            act.dma_start(par_rows[PG:PG + 16, :], norm_g.rearrange("l (k p) -> (l k) p", p=P)).then_inc(consts_loaded, 16)
            act.dma_start(par_rows[PW:PW + 48, :], conv_w.rearrange("l w (k p) -> (l w k) p", p=P)).then_inc(consts_loaded, 16)
            act.dma_start(par_rows[PF:PF + 8, :], final_g.rearrange("(k p) -> k p", p=P)).then_inc(consts_loaded, 16)
            act.dma_start(par_rows[PS:PS + 32, :], state_conv.rearrange("l b r (k p) -> (l b r k) p", p=P)).then_inc(consts_loaded, 16)
            for c in range(NCH + 1):
                act.wait_ge(rows_loaded[c], 16)
                _, n = chunk_cols(c)
                src = x_rows[:, c, :] if c < NCH else T0[0:DEC, 0:D]
                nc.scalar.activation(row_squares[0:n, c, :], src, ACT.Square, accum_out=sums[0:n, c:c + 1]).then_inc(rows_squared, 1)
                if c % 2 == 0:
                    act.wait_ge(rows_turned, c + 1)
                    a, n = chunk_cols(c)
                    nc.scalar.activation(x[:, :, a:a + n], psf[:, 0:KT * n].rearrange("p (k n) -> p k n", k=KT),
                                         ACT.Copy).then_inc(x_cols_act, 1)
            act.wait_ge(params_turned, 1)
            nc.scalar.activation(par[:, :], ps[:, 6, 0:NPAR], ACT.Copy).then_inc(params_ready, 1)

            def square(k8, m):
                act.wait_ge(ssq_added, k8 + m + OPEN)
                nc.scalar.activation(T0[:, :], x[:, ds(m, 1), :].rearrange("p a n -> p (a n)"), ACT.Square).then_inc(squared, 1)

            rstd_cols = psf[:, 3 * BANK:3 * BANK + COLS]

            def copy_rstd(k):
                act.wait_ge(rstd_spread, k + 1)
                nc.scalar.activation(rstd_row[:, :], rstd_cols, ACT.Copy).then_inc(rstd_copied, 1)

            def output_high(b):
                act.wait_ge(small_read, b + 1 + OPEN)
                nc.scalar.activation(o_hi[:, :, SAMP:TAIL], T1s, ACT.Copy).then_inc(o_hi_ready, 1)
                for v in range(2):
                    act.wait_ge(small_read, b + v + 2 + OPEN)
                    nc.scalar.activation(o_hi[:, v, 0:SEQ], T1[:, 0:SEQ], ACT.Copy).then_inc(o_hi_ready, 1)

            def head(l, h):
                _, u2, bb = head_bases(l, h)
                first = isinstance(h, int)
                n = l * HEADS + h
                b0 = bb if first else bb + 3
                uv = 2 if first else 10

                def unit(j):
                    act.wait_ge(unit_done, u2 * 2 + j + 1 + OPEN)

                def batch(b):
                    act.wait_ge(small_done, b + 1)

                act.wait_ge(small_read, bb + OPEN)
                act.dma_start(hc[:, :], head_c[ds(h, 1)].rearrange("a p n -> (a p) n")).then_inc(head_loaded, 16)
                act.wait_ge(states_stored, n * 32 + OPEN)
                act.dma_start(S[:, NCH + 1, :], state_ret[ds(l, 1), 0, ds(h, 1)].rearrange("a b p n -> (a b p) n")).then_inc(state_loaded, 16)

                def swap(j, scale):
                    unit(j)
                    act.wait_ge(roped, n * 2 + j + OPEN)
                    nc.scalar.activation(cols(T0[0:64, :]), slot(j)[64:128], ACT.Copy, scale=scale).then_inc(swapped, 1)

                if not first:
                    output_high(bb)
                swap(0, DK ** -0.5)
                swap(1, 1.0)
                batch(b0 + B_KT)
                act.wait_ge(head_loaded, n * 16 + 16)
                nc.scalar.activation(K[:, 0:NCH, :], small_k, ACT.Identity, scale=hc[:, KDEC:KDEC + 1]).then_inc(small_read, 1)
                for v, t in enumerate((T0[:, :], T1)):
                    unit(uv + v)
                    if v == 0:
                        act.wait_ge(roped, n * 2 + 2 + OPEN)
                    else:
                        act.wait_ge(o_split, n * 3 + OPEN)
                    nc.scalar.activation(cols(t), slot(v), ACT.Copy).then_inc(slot_read[v], 1)
                    batch(b0 + B_V0 + v)
                    nc.scalar.activation(V[:, 0:NCH, v * P:(v + 1) * P], small_k, ACT.Copy).then_inc(small_read, 1)
                batch(b0 + B_X)
                nc.scalar.activation(K[0:DEC, NCH, :], k_s, ACT.Identity, scale=hc[0:DEC, KDECS:KDECS + 1])
                nc.scalar.activation(V[0:DEC, NCH, :], v_s, ACT.Copy).then_inc(sample_copied, 1)
                unit(uv + 2)
                nc.scalar.activation(cols(zs[:, 0, :]), slot(0), ACT.Sigmoid).then_inc(z_gate, 1)
                batch(b0 + B_S)
                nc.scalar.activation(junk[0][0:DEC, :], small_v[0:DEC, 2, :], ACT.Square, accum_out=sums[0:DEC, 8:9]).then_inc(o_squared, 1)
                for g in range(2):
                    batch(b0 + B_OA + g)
                    for c in range(4):
                        i = nc.scalar.activation(junk[c][:, :], small_v[:, c, :], ACT.Square, accum_out=sums[:, 4 * g + c:4 * g + c + 1])
                    i.then_inc(o_squared, 1)
                    if g == 0:
                        unit(uv + 3)
                        nc.scalar.activation(cols(zs[:, 1, :]), slot(1), ACT.Sigmoid).then_inc(z_gate, 1)
                act.wait_ge(sample_state, n + 1)
                act.dma_start(ret_p[ds(l, 1), 0, ds(h, 1)].rearrange("a b p n -> (a b p) n"), S[:, NCH - 1, :]).then_inc(states_stored, 16)
                act.dma_start(ret_s[ds(l, 1), 0, ds(h, 1)].rearrange("a b p n -> (a b p) n"), S[:, NCH, :]).then_inc(states_stored, 16)

            with act.Fori(0, LAYERS) as l:
                copy_rstd(l)
                for m in range(KT):
                    act.wait_ge(normed, l * KT + m + 1)
                    nc.scalar.activation(act_hi[:, m, :], (T0[:, :], T1)[m % 2], ACT.Copy).then_inc(h_hi_ready, 1)
                act.wait_ge(x_stored, l * 64 + 64)
                act.wait_ge(h_ready, l * KT + KT)
                head(l, 0)
                with act.Fori(1, HEADS) as h:
                    head(l, h)
                output_high(l * BL + BL - 3)
                for j in range(2):
                    act.wait_ge(unit_done, l * UL + U_GR - 8 + j + 1 + OPEN)
                    act.wait_ge(o_split, (l * HEADS + HEADS) * 3 + OPEN)
                    nc.scalar.activation(cols((T0[:, :], T1)[j]), slot(j), ACT.Sigmoid).then_inc(slot_read[j], 1)
                with act.Fori(1, KT // 2) as i:
                    for j in range(2):
                        act.wait_ge(unit_done, l * UL + U_GR + i * 2 + j + 1 + OPEN)
                        act.wait_ge(r_gated, l * KT + i * 2 + j + OPEN)
                        nc.scalar.activation(cols((T0[:, :], T1)[j]), slot(j), ACT.Sigmoid).then_inc(slot_read[j], 1)
                act.wait_ge(r_gated, l * KT + KT + OPEN)
                act.wait_ge(states_stored, (l + 1) * (32 * HEADS) + OPEN)
                with act.Fori(0, KT) as m:
                    t = l * KT + m
                    u2 = l * (UL // 2) + U_A // 2 + m * 2
                    act.wait_ge(unit_done, u2 * 2 + 1 + OPEN)
                    act.wait_ge(a_split, t + OPEN)
                    nc.scalar.activation(cols(T0[:, :]), slot(0), ACT.Copy).then_inc(slot_read[0], 1)
                    act.wait_ge(u_ready, t + 1)
                    nc.scalar.activation(T0[:, :], T1, ACT.Identity, scale=par[:, ds(l * 24 + m + (PW + 16), 1)]).then_inc(conv_first, 1)
                    act.wait_ge(unit_done, u2 * 2 + 4 + OPEN)
                    act.wait_ge(conv_third, t + 1)
                    nc.scalar.activation(cols(T1), slot(1), ACT.Sigmoid).then_inc(a_gate, 1)
                    act.wait_ge(a_product, t + 1)
                    nc.scalar.activation(prod_hi[:, ds(m, 1), :].rearrange("p a n -> p (a n)"), T0[:, :], ACT.Copy).then_inc(a_hi_ready, 1)
                act.wait_ge(a_split, l * KT + KT + OPEN)

                def gate_a(l, m):
                    act.wait_ge(unit_done, l * UL + U_AG + m * 2 + 1 + OPEN)
                    act.wait_ge(merged, l * KT + m + OPEN)
                    nc.scalar.activation(cols(T0[:, :]), slot(0), ACT.Sigmoid).then_inc(slot_read[0], 1)

                with act.Fori(0, KT - 1) as m:
                    gate_a(l, m)
                gate_a(l, KT - 1)
                for m in range(KT):
                    act.wait_ge(merged, l * KT + m + 1 + OPEN)
                    nc.scalar.activation(act_hi[:, m, :], r[:, m, :], ACT.Copy).then_inc(m_hi_ready, 1)
                with act.Fori(0, KT // 2) as i:
                    for j in range(2):
                        act.wait_ge(slot_read[j], l * (UL // 2) + U_O // 2 + i + 1 + OPEN)
                        square(l * KT, i * 2 + j)

        @block.vector
        def _(dve):
            V_ = nc.vector
            for free in (small_read, slot_read[0], slot_read[1], roped, ssq_added, r_gated, a_split, merged, o_split):
                dve.sem_inc(free, OPEN)
            V_.memset(x[:, :, GAP:SAMP], 0.0).then_inc(gaps_set, 1)
            V_.memset(x[:, :, TAIL:COLS], 0.0).then_inc(gaps_set, 1)
            V_.memset(means[:, :], 1.0).then_inc(gaps_set, 1)
            for c in range(1, NCH + 1, 2):
                dve.wait_ge(rows_turned, c + 1)
                a, n = chunk_cols(c)
                V_.tensor_copy(x[:, :, a:a + n], psf[:, 3 * BANK:3 * BANK + KT * n].rearrange("p (k n) -> p k n", k=KT)).then_inc(x_cols_dve, 1)
            dve.wait_ge(rows_squared, NCH + 1)
            V_.tensor_scalar(means[:, 0:NCH], sums[:, 0:NCH], 1.0 / D, EPS, ALU.mult, ALU.add)
            V_.tensor_scalar(means[0:DEC, 8:9], sums[0:DEC, 8:9], 1.0 / D, EPS, ALU.mult, ALU.add).then_inc(mean_ready, 1)
            dve.wait_ge(params_ready, 1)
            V_.memset(U[:, 0:2], 0.0).then_inc(u_cleared, 1)
            dve.wait_ge(rows_turned, NCH + 1)

            def add_squares(l, m):
                dve.wait_ge(squared, l * KT + m + 1)
                dve.wait_ge(ssq_added, l * KT + m + OPEN)
                V_.tensor_tensor(T1, T1, T0[:, :], ALU.add).then_inc(ssq_added, 1)

            def norm_means(l):
                dve.wait_ge(norm_summed, l + 1)
                V_.tensor_scalar(means[:, 0:NCH], ps[:, 6, 0:NCH], 1.0 / D, EPS, ALU.mult, ALU.add)
                V_.tensor_scalar(means[0:DEC, 8:9], ps[0:DEC, 6, 8:9], 1.0 / D, EPS, ALU.mult, ALU.add).then_inc(mean_ready, 1)

            def norm_scale(l):
                dve.wait_ge(norm_power, l + 1)
                V_.tensor_tensor(T0[:, 0:SEQ].rearrange("p (c n) -> p c n", n=P), I[:, None, :].to_broadcast([P, NCH, P]),
                                 power[:, 0:NCH, None].to_broadcast([P, NCH, P]), ALU.mult)
                V_.tensor_scalar(T0[0:DEC, GAP:COLS], ident[0:DEC, 0:DEC + 4], power[0:DEC, 8:9], None, ALU.mult).then_inc(diag_ready, 1)

            def gated_output(hn, b):
                dve.wait_ge(small_done, b + 1)
                V_.tensor_tensor(T1s, o_s, zs[:, :, SAMP:TAIL], ALU.mult).then_inc(small_read, 1)
                dve.wait_ge(o_hi_ready, hn * 3 + 1)
                V_.tensor_tensor(o_lo[:, :, SAMP:TAIL], T1s, o_hi[:, :, SAMP:TAIL].bitcast(F32), ALU.subtract).then_inc(o_split, 1)
                for v in range(2):
                    dve.wait_ge(small_done, b + v + 2)
                    dve.wait_ge(o_split, hn * 3 + v + 1 + OPEN)
                    V_.tensor_tensor(T1[:, 0:SEQ], small, zs[:, v, 0:SEQ], ALU.mult).then_inc(small_read, 1)
                    dve.wait_ge(o_hi_ready, hn * 3 + v + 2)
                    V_.tensor_tensor(o_lo[:, v, 0:SEQ], T1[:, 0:SEQ], o_hi[:, v, 0:SEQ].bitcast(F32), ALU.subtract).then_inc(o_split, 1)

            def head(l, h):
                _, u2, bb = head_bases(l, h)
                first = isinstance(h, int)
                n = l * HEADS + h
                b0 = bb if first else bb + 3
                uv = 2 if first else 10

                def unit(j):
                    dve.wait_ge(unit_done, u2 * 2 + j + 1 + OPEN)

                def batch(b):
                    dve.wait_ge(small_done, b + 1)

                def rotate(j, out, scale):
                    unit(j)
                    dve.wait_ge(roped, n * 2 + j + OPEN)
                    V_.tensor_scalar(cols(T0[64:128, :]), slot(j)[0:64], scale, None, ALU.mult)
                    dve.wait_ge(swapped, n * 2 + j + 1)
                    V_.scalar_tensor_tensor(cols(out[:, :]), slot(j), scale, cols(rope[:, 0, :]), ALU.mult, ALU.mult).then_inc(slot_read[j], 1)
                    dve.wait_ge(slot_read[j], u2 + 1 + OPEN)
                    V_.tensor_tensor(T0[:, :], T0[:, :], rope[:, 1, :], ALU.mult).then_inc(swapped_sin, 1)
                    dve.wait_ge(swapped_sin, n * 2 + j + 1)
                    V_.tensor_tensor(out[:, :], out[:, :], T0[:, :], ALU.add).then_inc(roped, 1)

                def add_r(w):
                    unit(2 + w)
                    V_.tensor_tensor(cols(r[:, w, :]), slot(w % 2), cols(r[:, w, :]), ALU.add).then_inc(slot_read[w % 2], 1)

                def scan(c, last):
                    if c == 0:
                        i = V_.tensor_copy(S[:, 0, :], small_v[:, 0, :])
                    else:
                        i = V_.scalar_tensor_tensor(S[:, c, :], S[:, c - 1, :], hc[:, G128:G128 + 1], small_v[:, c % 4, :], ALU.mult, ALU.add)
                    i.then_inc(small_read if last else scanned, 1)

                def normalise(k, rows, c0, nch, src):
                    dve.wait_ge(o_squared, n * 3 + k + 1)
                    V_.tensor_scalar(means[0:rows, c0:c0 + nch], sums[0:rows, c0:c0 + nch], hc[0:rows, OA_:OA_ + 1], EPS, ALU.mult, ALU.add).then_inc(o_mean, 1)
                    dve.wait_ge(o_power, n * 3 + k + 1)
                    V_.tensor_scalar(rstds[0:rows, c0:c0 + nch], power[0:rows, c0:c0 + nch], hc[0:rows, OB_:OB_ + 1], None, ALU.mult).then_inc(o_rstd, 1)
                    dve.wait_ge(o_rstd, n * 3 + k + 1)
                    V_.tensor_tensor(V[0:rows, c0:c0 + nch, :], src, rstds[0:rows, c0:c0 + nch, None].to_broadcast([rows, nch, DV]), ALU.mult).then_inc(small_read, 1)

                dve.wait_ge(rope_loaded, l * 16 + 16)
                if not first:
                    dve.wait_ge(slot_read[1], u2 + OPEN)
                    gated_output(n - 1, bb)
                rotate(0, kT, DK ** -0.5)
                rotate(1, qT, 1.0)
                if not first:
                    for w in range(KT):
                        add_r(w)
                batch(b0 + B_SC)
                dve.wait_ge(head_loaded, n * 16 + 16)
                V_.tensor_tensor(Pr[:, 0:NCH, :], small_k, hc[:, None, MASK:MASK + CHUNK].to_broadcast([P, NCH, CHUNK]), ALU.mult).then_inc(small_read, 1)
                batch(b0 + B_X)
                dve.wait_ge(sample_copied, n + 1)
                V_.tensor_tensor(Pr[0:DEC, NCH, 0:DEC], score_s, hc[0:DEC, MASK:MASK + DEC], ALU.mult).then_inc(small_read, 1)

                def silu(v):
                    unit(uv + 2 + v)
                    dve.wait_ge(z_gate, n * 2 + v + 1)
                    V_.tensor_tensor(cols(zs[:, v, :]), slot(v), cols(zs[:, v, :]), ALU.mult).then_inc(slot_read[v], 1)

                batch(b0 + B_KVA)
                for c in range(4):
                    if c:
                        dve.wait_ge(scanned, n * 6 + c)
                    scan(c, c == 3)
                silu(0)
                batch(b0 + B_KVB)
                dve.wait_ge(small_read, b0 + B_KVA + 1 + OPEN)
                for c in range(4, 8):
                    if c > 4:
                        dve.wait_ge(scanned, n * 6 + c - 1)
                    scan(c, c == 7)
                batch(b0 + B_S)
                dve.wait_ge(state_loaded, n * 16 + 16)
                V_.scalar_tensor_tensor(S[:, NCH, :], S[:, NCH + 1, :], hc[:, G64:G64 + 1], small_v[:, 0, :], ALU.mult, ALU.add).then_inc(sample_state, 1)
                normalise(0, DEC, 8, 1, small_v[0:DEC, 2:3, :])
                batch(b0 + B_OA)
                normalise(1, P, 0, 4, small_v)
                silu(1)
                batch(b0 + B_OB)
                normalise(2, P, 4, 4, small_v)

            with dve.Fori(0, LAYERS) as l:
                norm_scale(l)
                dve.wait_ge(rstd_copied, l + 1)

                def normal_tile(m):
                    V_.scalar_tensor_tensor((T0[:, :], T1)[m % 2], x[:, m, :], par[:, ds(l * KT + m + PG, 1)], rstd_row[:, :], ALU.mult, ALU.mult).then_inc(normed, 1)

                normal_tile(0)
                for m in range(KT):
                    if m + 1 < KT:
                        if m:
                            dve.wait_ge(h_ready, l * KT + m)
                        normal_tile(m + 1)
                    dve.wait_ge(h_hi_ready, l * KT + m + 1)
                    V_.tensor_tensor(act_lo[:, m, :], (T0[:, :], T1)[m % 2], act_hi[:, m, :].bitcast(F32), ALU.subtract).then_inc(h_ready, 1)
                V_.memset(r[:, :, :], 0.0).then_inc(r_cleared, 1)
                dve.wait_ge(x_stored, l * 64 + 64)
                for half in (o_hi, o_lo):
                    V_.memset(half[:, :, GAP:SAMP].bitcast(F32), 0.0)
                    V_.memset(half[:, :, TAIL:COLS].bitcast(F32), 0.0).then_inc(r_cleared, 1)
                head(l, 0)
                with dve.Fori(1, HEADS) as h:
                    head(l, h)
                dve.wait_ge(slot_read[1], l * (UL // 2) + (U_GR - 8) // 2 + OPEN)
                gated_output(l * HEADS + HEADS - 1, l * BL + BL - 3)
                for w in range(KT):
                    dve.wait_ge(unit_done, l * UL + U_GR - 6 + w + 1 + OPEN)
                    V_.tensor_tensor(cols(r[:, w, :]), slot(w % 2), cols(r[:, w, :]), ALU.add).then_inc(slot_read[w % 2], 1)
                for j in range(2):
                    dve.wait_ge(slot_read[j], l * (UL // 2) + (U_GR - 8) // 2 + 5 + OPEN)
                    V_.tensor_tensor(r[:, j, :], r[:, j, :], (T0[:, :], T1)[j], ALU.mult).then_inc(r_gated, 1)
                with dve.Fori(1, KT // 2) as i:
                    for j in range(2):
                        dve.wait_ge(slot_read[j], l * (UL // 2) + U_GR // 2 + i + 1 + OPEN)
                        rm = r[:, ds(i * 2 + j, 1), :].rearrange("p a n -> p (a n)")
                        V_.tensor_tensor(rm, rm, (T0[:, :], T1)[j], ALU.mult).then_inc(r_gated, 1)
                with dve.Fori(0, KT) as m:
                    t = l * KT + m
                    u2 = l * (UL // 2) + U_A // 2 + m * 2
                    dve.wait_ge(unit_done, u2 * 2 + 2 + OPEN)
                    dve.wait_ge(slot_read[0], u2 + 1 + OPEN)
                    V_.tensor_tensor(cols(T1), slot(1), cols(T0[:, :]), ALU.mult).then_inc(slot_read[1], 1)
                    dve.wait_ge(slot_read[1], u2 + 1 + OPEN)
                    dve.wait_ge(conv_stored, l * 64 + OPEN)
                    V_.tensor_copy(conv_keep[:, 0, :, ds(m, 1)].rearrange("p r a -> p (r a)"), T1[:, SEQ - 2:SEQ])
                    V_.tensor_copy(conv_keep[:, 1, :, ds(m, 1)].rearrange("p r a -> p (r a)"), T1[:, TAIL - 2:TAIL]).then_inc(conv_kept, 1)
                    V_.tensor_copy(T1[:, GAP:GAP + 1], par[:, ds(l * 16 + m + PS, 1)])
                    V_.tensor_copy(T1[:, GAP + 1:GAP + 2], par[:, ds(l * 16 + m + (PS + 8), 1)]).then_inc(u_ready, 1)
                    dve.wait_ge(conv_first, t + 1)
                    V_.scalar_tensor_tensor(T0[:, :], U[:, 1:1 + COLS], par[:, ds(l * 24 + m + (PW + 8), 1)], T0[:, :], ALU.mult, ALU.add).then_inc(conv_second, 1)
                    dve.wait_ge(conv_second, t + 1)
                    V_.scalar_tensor_tensor(T0[:, :], U[:, 0:COLS], par[:, ds(l * 24 + m + PW, 1)], T0[:, :], ALU.mult, ALU.add).then_inc(conv_third, 1)
                    dve.wait_ge(unit_done, u2 * 2 + 3 + OPEN)
                    dve.wait_ge(conv_third, t + 1)
                    V_.tensor_tensor(cols(T0[:, :]), slot(0), cols(T0[:, :]), ALU.mult).then_inc(slot_read[0], 1)
                    dve.wait_ge(a_gate, t + 1)
                    dve.wait_ge(slot_read[0], u2 + 2 + OPEN)
                    V_.tensor_tensor(cols(T0[:, :]), slot(1), cols(T0[:, :]), ALU.mult).then_inc(slot_read[1], 1)
                    dve.wait_ge(slot_read[1], u2 + 2 + OPEN)
                    V_.tensor_tensor(T0[:, :], T0[:, :], T1, ALU.mult).then_inc(a_product, 1)
                    dve.wait_ge(a_hi_ready, t + 1)
                    V_.tensor_tensor(prod_lo[:, ds(m, 1), :].rearrange("p a n -> p (a n)"), T0[:, :],
                                     prod_hi[:, ds(m, 1), :].rearrange("p a n -> p (a n)").bitcast(F32), ALU.subtract).then_inc(a_split, 1)

                def merge(l, m, rm):
                    u2 = l * (UL // 2) + U_AG // 2 + m
                    dve.wait_ge(unit_done, u2 * 2 + 2 + OPEN)
                    dve.wait_ge(slot_read[0], u2 + 1 + OPEN)
                    V_.tensor_tensor(cols(T1), slot(1), cols(T0[:, :]), ALU.mult).then_inc(slot_read[1], 1)
                    dve.wait_ge(slot_read[1], u2 + 1 + OPEN)
                    V_.tensor_tensor(rm, rm, T1, ALU.add).then_inc(merged, 1)

                def merged_low(m):
                    dve.wait_ge(m_hi_ready, l * KT + m + 1)
                    V_.tensor_tensor(act_lo[:, m, :], r[:, m, :], act_hi[:, m, :].bitcast(F32), ALU.subtract).then_inc(m_split, 1)

                with dve.Fori(0, KT - 1) as m:
                    merge(l, m, r[:, ds(m, 1), :].rearrange("p a n -> p (a n)"))
                for m in range(KT - 1):
                    merged_low(m)
                merge(l, KT - 1, r[:, KT - 1, :])
                merged_low(KT - 1)
                V_.memset(T1, 0.0).then_inc(ssq_cleared, 1)
                dve.wait_ge(ssq_cleared, l + 1)
                for g in range(4):
                    dve.wait_ge(x_loaded[g], l * 16 + 16)
                    for j in range(2):
                        m = 2 * g + j
                        dve.wait_ge(unit_done, l * UL + U_O + m + 1 + OPEN)
                        V_.tensor_tensor(cols(x[:, m, :]), slot(j), cols(x[:, m, :]), ALU.add).then_inc(slot_read[j], 1)
                        add_squares(l, m)
                norm_means(l)
            dve.wait_ge(norm_power, LAYERS + 1)
            dve.wait_ge(g_loaded, 16)
            for c in range(NCH + 1):
                dve.wait_ge(y_turned, c + 1)
                n = P if c < NCH else DEC
                a = 3 * BANK * (c % 2)
                V_.scalar_tensor_tensor(y_rows[0:n, c, :], psf[0:n, a:a + D], power[0:n, c:c + 1], g_rows[0:n, :],
                                        ALU.mult, ALU.mult).then_inc(y_read, 1)

        @block.tensor
        def _(pe):
            mm = nc.tensor.matmul
            pe.sem_inc(weights_started, OPEN)
            pe.sem_inc(unit_done, OPEN)
            pe.wait_ge(ident_loaded, 16)
            for c in range(NCH + 1):
                pe.wait_ge(rows_loaded[c], 16)
                if c >= 2:
                    pe.wait_ge((x_cols_act, x_cols_dve)[c % 2], c // 2)
                _, n = chunk_cols(c)
                src = x_rows[:, c, :] if c < NCH else T0[0:DEC, 0:D]
                for k in range(KT):
                    a = 3 * BANK * (c % 2) + k * n
                    i = nc.tensor.transpose(psf[:, a:a + n], src[:, k * P:(k + 1) * P], I[0:n, 0:n])
                i.then_inc(rows_turned, 1)
            pe.wait_ge(consts_loaded, 64)
            nc.tensor.transpose(ps[:, 6, 0:NPAR], par_rows[0:NPAR, :], I[0:NPAR, 0:NPAR]).then_inc(params_turned, 1)
            pe.wait_ge(ones_set, 1)

            def norm_sums(l):
                pe.wait_ge(ssq_added, l * KT + KT + OPEN)
                for c in range(NCH + 1):
                    a, n = chunk_cols(c)
                    i = mm(ps[0:n, 6, c:c + 1], T1[:, a:a + n], ones[:, 0:1], start=True, stop=True)
                i.then_inc(norm_summed, 1)

            def norm_spread(l):
                pe.wait_ge(diag_ready, l + 1)
                for c in range(NCH):
                    mm(psf[:, 3 * BANK + c * P:3 * BANK + (c + 1) * P], ones[:, :], T0[:, c * P:(c + 1) * P], start=True, stop=True)
                mm(psf[:, 5 * BANK:5 * BANK + DEC + 4], ones[0:DEC, :], T0[0:DEC, GAP:COLS], start=True, stop=True).then_inc(rstd_spread, 1)

            def tile_products(s, ws, hi, lo, k, ktiles, a):
                terms = ((w_hi[ws], hi), (w_hi[ws], lo), (w_lo[ws], hi))
                done = []
                for t, (w, b) in enumerate(terms):
                    for c in range(3):
                        done.append(mm(ps[:, 3 * s + c, 0:THIRD], w[:, a:a + P], b[:, k, c * THIRD:(c + 1) * THIRD],
                                       start=(k == 0 and t == 0), stop=(k == ktiles - 1 and t == 2)))
                return done

            def unit(n, u2, s, hi=act_hi, lo=act_lo, between={}, ready=None):
                pe.wait_ge(weights_split, n + 1)
                pe.wait_ge(slot_read[s], u2 + OPEN)
                for k in range(KT):
                    if k in between:
                        between[k]()
                    if ready is not None:
                        ready(k)
                    done = tile_products(s, s, hi, lo, k, KT, k * P)
                    if k == 0:
                        done[0].then_inc(weights_started, 1)
                done[-1].then_inc(unit_done, 1)

            def first_units(l):
                for s in range(2):
                    pe.wait_ge(weights_split, l * WL + s + 1)
                    pe.wait_ge(rstd_copied, l + 1)
                    pe.wait_ge(slot_read[s], l * (UL // 2) + OPEN)
                for k in range(KT):
                    pe.wait_ge(h_ready, l * KT + k + 1)
                    for s in range(2):
                        done = tile_products(s, s, act_hi, act_lo, k, KT, k * P)
                        if k == (0, KT - 1)[s]:
                            done[0].then_inc(weights_started, 1)
                        if k == KT - 1:
                            done[-1].then_inc(unit_done, 1)

            def w_r_unit(n0, u2, w, o_ready):
                if w % 4 == 0:
                    pe.wait_ge(weights_split, n0 + w // 4 + 1)
                if w == 0:
                    pe.wait_ge(o_split, o_ready + OPEN)
                pe.wait_ge(slot_read[w % 2], u2 + w // 2 + OPEN)
                for k in range(2):
                    done = tile_products(w % 2, w // 4, o_hi, o_lo, k, 2, (w % 4) * P + k * 512)
                    if k == 0 and w % 4 == 0:
                        done[0].then_inc(weights_started, 1)
                done[-1].then_inc(unit_done, 1)

            def turn_output_sample(b):
                pe.wait_ge(small_read, b + OPEN)
                for v in range(2):
                    i = mm(o_s[:, v, :], V[0:DEC, NCH, v * P:(v + 1) * P], I[0:DEC, 0:DEC], start=True, stop=True)
                i.then_inc(small_done, 1)

            def turn_output(v, b):
                pe.wait_ge(small_read, b + OPEN)
                for c in range(NCH):
                    i = nc.tensor.transpose(small_k[:, c, :], V[:, c, v * P:(v + 1) * P], I)
                i.then_inc(small_done, 1)

            def output_batches(bb):
                return {4: lambda: turn_output_sample(bb), 5: lambda: turn_output(0, bb + 1),
                        7: lambda: turn_output(1, bb + 2)}

            def head(l, h):
                n0, u2, bb = head_bases(l, h)
                first = isinstance(h, int)
                n = l * HEADS + h
                b0 = bb if first else bb + 3
                n1, u1 = (n0 + 2, u2 + 1) if first else (n0 + 4, u2 + 5)

                def turn_keys():
                    pe.wait_ge(small_read, b0 + B_KT + OPEN)
                    pe.wait_ge(roped, n * 2 + 1 + OPEN)
                    for c in range(NCH):
                        i = nc.tensor.transpose(small_k[:, c, :], kT[:, c * CHUNK:(c + 1) * CHUNK], I)
                    i.then_inc(small_done, 1)

                def scores():
                    pe.wait_ge(small_read, b0 + B_SC + OPEN)
                    pe.wait_ge(roped, n * 2 + 2 + OPEN)
                    for c in range(NCH):
                        a = c * CHUNK
                        i = mm(small_k[:, c, :], kT[:, a:a + CHUNK], qT[:, a:a + CHUNK], start=True, stop=True)
                    i.then_inc(small_done, 1)

                def turn_values(v):
                    pe.wait_ge(small_read, b0 + B_V0 + v + OPEN)
                    pe.wait_ge(slot_read[v], u1 + 1 + OPEN)
                    for c in range(NCH):
                        i = nc.tensor.transpose(small_k[:, c, :], (T0[:, :], T1)[v][:, c * CHUNK:(c + 1) * CHUNK], I)
                    i.then_inc(small_done, 1)

                def sample_batch():
                    pe.wait_ge(small_read, b0 + B_X + OPEN)
                    mm(score_s, kT[:, SAMP:TAIL], qT[:, SAMP:TAIL], start=True, stop=True)
                    nc.tensor.transpose(k_s, kT[:, SAMP:TAIL], I)
                    for v, src in enumerate((T0[:, :], T1)):
                        i = nc.tensor.transpose(v_s[:, v * P:(v + 1) * P], src[:, SAMP:TAIL], I)
                    i.then_inc(small_done, 1)

                def keys_by_values(g):
                    pe.wait_ge(small_read, b0 + B_KVA + g + OPEN)
                    for c in range(4):
                        i = mm(small_v[:, c, :], K[:, 4 * g + c, :], V[:, 4 * g + c, :], start=True, stop=True)
                    i.then_inc(small_done, 1)

                def sample_output():
                    pe.wait_ge(small_read, b0 + B_S + OPEN)
                    pe.wait_ge(state_loaded, n * 16 + 16)
                    mm(small_v[:, 0, :], K[0:DEC, NCH, :], V[0:DEC, NCH, :], start=True, stop=True)
                    mm(small_v[0:DEC, 2, :], Pr[0:DEC, NCH, 0:DEC], V[0:DEC, NCH, :], start=True, stop=False)
                    mm(small_v[0:DEC, 2, :], qT[:, SAMP:TAIL], S[:, NCH + 1, :], start=False, stop=True).then_inc(small_done, 1)

                def outputs(g):
                    pe.wait_ge(small_read, b0 + B_OA + g + OPEN)
                    for c in range(4 * g, 4 * g + 4):
                        i = mm(small_v[:, c % 4, :], Pr[:, c, :], V[:, c, :], start=True, stop=c == 0)
                        if c:
                            i = mm(small_v[:, c % 4, :], qT[:, c * CHUNK:(c + 1) * CHUNK], S[:, c - 1, :], start=False, stop=True)
                    i.then_inc(small_done, 1)

                if first:
                    first_units(l)
                else:
                    unit(n0, u2, 0, between=output_batches(bb))
                    unit(n0 + 1, u2, 1)
                    for w in range(KT):
                        w_r_unit(n0 + 2, u2 + 1, w, n * 3)
                unit(n1, u1, 0, between={5: turn_keys, 7: scores} if first else {2: turn_keys, 6: scores})
                unit(n1 + 1, u1, 1, between={3: lambda: turn_values(0)})
                unit(n1 + 2, u1 + 1, 0, between={2: lambda: turn_values(1), 4: sample_batch, 6: lambda: keys_by_values(0)})
                unit(n1 + 3, u1 + 1, 1, between={0: lambda: keys_by_values(1), 2: sample_output, 4: lambda: outputs(0)})
                outputs(1)

            with pe.Fori(0, LAYERS) as l:
                norm_spread(l)
                head(l, 0)
                with pe.Fori(1, HEADS) as h:
                    head(l, h)
                for j in range(2):
                    unit(l * WL + W_GR - 2 + j, l * (UL // 2) + (U_GR - 8) // 2, j,
                         between=output_batches(l * BL + BL - 3) if j == 0 else {})
                for w in range(KT):
                    w_r_unit(l * WL + W_GR, l * (UL // 2) + (U_GR - 6) // 2, w, (l * HEADS + HEADS) * 3)
                with pe.Fori(1, KT // 2) as i:
                    for j in range(2):
                        unit(l * WL + W_GR + i * 2 + j, l * (UL // 2) + U_GR // 2 + i, j)
                with pe.Fori(0, KT) as m:
                    for j in range(4):
                        unit(l * WL + W_A + m * 4 + j, l * (UL // 2) + U_A // 2 + m * 2 + j // 2, j % 2)
                with pe.Fori(0, KT) as m:
                    unit(l * WL + W_AG + m * 2, l * (UL // 2) + U_AG // 2 + m, 0)
                    pe.wait_ge(a_split, l * KT + KT + OPEN)
                    unit(l * WL + W_AG + m * 2 + 1, l * (UL // 2) + U_AG // 2 + m, 1, prod_hi, prod_lo)
                for j in range(2):
                    unit(l * WL + W_O + j, l * (UL // 2) + U_O // 2, j,
                         ready=(lambda k: pe.wait_ge(m_split, l * KT + k + 1)) if j == 0 else None)
                with pe.Fori(1, KT // 2) as i:
                    for j in range(2):
                        unit(l * WL + W_O + i * 2 + j, l * (UL // 2) + U_O // 2 + i, j)
                norm_sums(l)
            for c in range(NCH + 1):
                if c >= 2:
                    pe.wait_ge(y_read, c - 1)
                a, n = chunk_cols(c)
                for k in range(KT):
                    o = 3 * BANK * (c % 2) + k * P
                    i = nc.tensor.transpose(psf[0:n, o:o + P], x[:, k, a:a + n], I)
                i.then_inc(y_turned, 1)


_INS = ["x_prompt", "x_sample", "state_conv", "state_ret", "norm_g", "w_in", "conv_w", "w_a", "w_r", "w_o", "final_g"]
_OUTS = [(1, SEQ, D), (1, DEC, D), (LAYERS, 1, 2, D), (LAYERS, 1, HEADS, DK, DV),
         (LAYERS, 1, 2, D), (LAYERS, 1, HEADS, DK, DV)]


def shape_constants(np):
    half = DK // 2
    pos = np.zeros(COLS, np.float32)
    pos[0:SEQ] = np.arange(SEQ)
    pos[SAMP:TAIL] = PAST + np.arange(DEC)
    inv = (1.0 / (10000.0 ** (np.arange(half, dtype=np.float32) / half))).astype(np.float32)
    ang = (inv[:, None] * pos[None, :]).astype(np.float32).astype(np.float64)
    rope = np.zeros((2, P, COLS), np.float32)
    rope[0, 0:half] = rope[0, half:] = np.cos(ang)
    rope[1, 0:half] = -np.sin(ang)
    rope[1, half:] = np.sin(ang)
    heads = np.zeros((HEADS, P, NHC), np.float32)
    i = np.arange(CHUNK, dtype=np.float64)
    for h in range(HEADS):
        g = 1.0 - 2.0 ** (-5.0 - h)
        heads[h, :, MASK:MASK + CHUNK] = np.where(i[None, :] >= i[:, None], g ** -(i[:, None] + 1), 0.0)
        heads[h, :, KDEC] = g ** (CHUNK - 1 - i)
        heads[h, 0:DEC, KDECS] = g ** (DEC - 1 - i[0:DEC])
        heads[h, :, OA_] = g ** (2 * (i + 1)) / DV
        heads[h, :, OB_] = g ** (i + 1)
        heads[h, :, G128] = g ** CHUNK
        heads[h, :, G64] = g ** DEC
    ident = np.zeros((P, P + 2), np.float32)
    ident[:, 2:] = np.eye(P, dtype=np.float32)
    return {"rope_c": rope, "head_c": heads, "ident_c": ident}


def kernel(**inputs):
    import numpy as _np
    import concourse.bacc as _bacc
    from concourse import mybir as _mybir
    from concourse.bass_utils import run_bass_kernel_spmd as _run

    nc = _bacc.Bacc("TRN2", target_bir_lowering=False, num_devices=1)
    arrays, args = {}, []
    for name in _INS:
        a = _np.ascontiguousarray(inputs[name])
        arrays[f"in_{name}_dram"] = a
        args.append(nc.dram_tensor(f"in_{name}_dram", a.shape, _mybir.dt.from_np(a.dtype), kind="ExternalInput").ap())
    for name, a in shape_constants(_np).items():
        arrays[name] = a
        args.append(nc.dram_tensor(name, a.shape, _mybir.dt.from_np(a.dtype), kind="ExternalInput").ap())
    for i, shape in enumerate(_OUTS):
        args.append(nc.dram_tensor(f"out_{i}_dram", shape, _mybir.dt.float32, kind="ExternalOutput").ap())
    args.append(nc.dram_tensor("x_keep", (P, KT, COLS), _mybir.dt.float32, kind="Internal").ap())
    build(nc, *args)
    r = _run(nc, [arrays], core_ids=[0])
    return tuple(r.results[0][f"out_{i}_dram"] for i in range(len(_OUTS)))
```

```python
import concourse.bass as bass
from concourse import mybir
from contextlib import ExitStack

F32 = mybir.dt.float32
F32R = mybir.dt.float32r
ALU = mybir.AluOpType
ACT = mybir.ActivationFunctionType
ds = bass.ds

P = 128
D = 1024
KT = D // P
SEQ, DEC, PAST = 1024, 64, 128
LAYERS = 2
HEADS, DK, DV = 4, 128, 256
CHUNK = 128
NCH = SEQ // CHUNK
SAMP = SEQ
TAIL = SAMP + DEC
COLS = TAIL + 4
U_SAMP = SEQ + 2
BANK = 512
THIRD = COLS // 3
LAST = TAIL - 2 * THIRD
EPS = 1e-6
OPEN = 1

Y_POOL = (2, 5)
Y_DVE = (0, 1, 3, 4, 6, 7, 8)

HC, B_, C_, ZA, Q_, K_, V_, ZR, GA, GR = 0, 1024, 2048, 3072, 4096, 4608, 5120, 6144, 7168, 8192

WL = 96
UL = 120
BL = 52
W_GR, W_A, W_AG, W_O = 32, 40, 72, 88
U_GR, U_A, U_AG, U_O = 56, 64, 96, 112

MASK, KDEC, KDECS, OA_, OB_, G128, G64 = 0, 128, 129, 130, 131, 132, 133
NHC = 134
PG, PW, PS = 0, 16, 64
NPAR = 96


def build(nc, x_prompt, x_sample, state_conv, state_ret, norm_g, w_in, conv_w, w_a, w_r, w_o, final_g,
          rope_c, head_c, ident_c, y_prompt, y_sample, conv_p, ret_p, conv_s, ret_s, x_keep):
    with ExitStack() as ctx:
        base = (nc.sbuf_base + 63) // 64 * 64
        size = 212 * 1024 - 5 * 1024
        at = [0]

        def place(name, shape, dtype, offset=None):
            n = 4
            for s in shape[1:]:
                n *= s
            if dtype == mybir.dt.bfloat16:
                n //= 2
            if offset is None:
                offset = at[0]
                at[0] += (n + 31) // 32 * 32
            return nc.alloc_sbuf_tensor_at(name, shape, dtype, offset=base + offset), (offset + n + 31) // 32 * 32

        TILE = COLS * 4
        act_hi, _ = place("act_hi", [P, KT, COLS], F32R)
        act_lo, _ = place("act_lo", [P, KT, COLS], F32R)
        y_rows, _ = place("y_rows", [P, NCH + 1, D], F32, offset=0)
        row_squares, _ = place("row_squares", [P, NCH + 1, D], mybir.dt.bfloat16, offset=0)
        r_at = at[0]
        r, _ = place("r", [P, KT, COLS], F32)
        x_rows, _ = place("x_rows", [P, NCH, D], F32, offset=r_at)
        area = at[0]
        at[0] += 2 * KT * TILE
        x, _ = place("x", [P, KT, COLS], F32, offset=area)
        prod_hi, e = place("prod_hi", [P, KT, COLS], F32R, offset=area)
        prod_lo, _ = place("prod_lo", [P, KT, COLS], F32R, offset=e)
        g_rows, _ = place("g_rows", [P, D], F32, offset=area + KT * TILE)
        o_hi, e = place("o_hi", [P, 2, COLS], F32R, offset=area)
        o_lo, e = place("o_lo", [P, 2, COLS], F32R, offset=e)
        K_lo, e2 = place("K_lo", [P, NCH, DK], F32R, offset=area)
        V_lo, e2 = place("V_lo", [P, NCH, DV], F32R, offset=e2)
        Pr_lo, e2 = place("Pr_lo", [P, NCH, CHUNK], F32R, offset=e2)
        assert e2 <= e
        S, e = place("S", [P, NCH + 2, DV], F32, offset=e)
        V_hi, _ = place("V_hi", [P, NCH, DV], F32R, offset=e)
        V, e = place("V", [P, NCH + 1, DV], F32, offset=e)
        K_hi, _ = place("K_hi", [P, NCH, DK], F32R, offset=e)
        K, e = place("K", [P, NCH + 1, DK], F32, offset=e)
        rstd_row, _ = place("rstd_row", [P, COLS], F32, offset=e)
        assert e >= area + KT * TILE
        Pr_hi, _ = place("Pr_hi", [P, NCH, CHUNK], F32R, offset=e)
        Pr, e = place("Pr", [P, NCH + 1, CHUNK], F32, offset=e)
        kT, _ = place("kT", [P, COLS], F32, offset=e)
        zs, e = place("zs", [P, 2, COLS], F32, offset=e)
        rope, e = place("rope", [P, 2, COLS], F32, offset=e)
        qT, e = place("qT", [P, COLS], F32, offset=e)
        junk = []
        for c in range(4):
            t, e2 = place(f"junk{c}", [P, DV], mybir.dt.bfloat16, offset=e if c < 3 else None)
            junk.append(t)
            e = e2 if c < 3 else e
        assert e <= area + 2 * KT * TILE
        w_raw = [place(f"w_raw{s}", [P, D], F32)[0] for s in range(2)]
        w_hi = [place(f"w_hi{s}", [P, D], F32R)[0] for s in range(2)]
        w_lo = [place(f"w_lo{s}", [P, D], F32R)[0] for s in range(2)]
        T0, _ = place("T0", [P, COLS], F32)
        t1_at = at[0]
        U, _ = place("U", [P, COLS + 4], F32)
        par_rows, _ = place("par_rows", [P, P], F32, offset=t1_at + 64)
        T1 = U[:, 2:2 + COLS]
        ident, _ = place("ident", [P, P], F32)
        ones, _ = place("ones", [P, P], F32)
        par, _ = place("par", [P, NPAR], F32)
        hc, _ = place("hc", [P, NHC], F32)
        conv_keep, _ = place("conv_keep", [P, 2, 2, KT], F32)
        sums, _ = place("sums", [P, 9], F32)
        means, _ = place("means", [P, 9], F32)
        power, _ = place("power", [P, 9], F32)
        rstds, _ = place("rstds", [P, 9], F32)
        neg_half, _ = place("neg_half", [P, 9], F32)
        zero, _ = place("zero", [P, 1], F32)
        assert at[0] <= nc.sbuf_usable_end - base, (at[0], nc.sbuf_usable_end - base)
        I = ident[:, :]

        ps = ctx.enter_context(nc.psum_tensor("ps", [P, 8, BANK], F32))
        psf = ps[:, :, :].rearrange("p b n -> p (b n)")

        def slot(s):
            return ps[:, 3 * s:3 * s + 3, 0:THIRD]

        def cols(a):
            return a.rearrange("p (c n) -> p c n", c=3)

        small = psf[:, 6 * BANK:8 * BANK]
        small_k = small.rearrange("p (c n) -> p c n", n=CHUNK)
        small_v = small.rearrange("p (c n) -> p c n", n=DV)
        k_s = ps[0:DEC, 6, 0:DK]
        v_s = ps[0:DEC, 6, DK:DK + DV]
        score_s = ps[0:DEC, 7, 0:DEC]
        o_s = ps[:, 6, 0:2 * DEC].rearrange("p (v n) -> p v n", v=2)
        T1s = T1[:, 0:2 * DEC].rearrange("p (v n) -> p v n", v=2)

        def sem(name):
            return ctx.enter_context(nc.semaphore(name))

        ident_loaded = sem("ident_loaded")
        consts_loaded = sem("consts_loaded")
        ones_set = sem("ones_set")
        rows_loaded = [sem(f"rows_loaded{c}") for c in range(NCH + 1)]
        unused_zeroed = sem("unused_zeroed")
        act_table = sem("act_table")
        params_turned = sem("params_turned")
        params_ready = sem("params_ready")
        rows_turned = sem("rows_turned")
        rows_squared = sem("rows_squared")
        u_cleared = sem("u_cleared")
        x_cols_act = sem("x_cols_act")
        x_cols_dve = sem("x_cols_dve")
        weights_loaded = [sem(f"weights_loaded{s}") for s in range(2)]
        weights_hi = sem("weights_hi")
        weights_split = sem("weights_split")
        weights_started = sem("weights_started")
        unit_done = sem("unit_done")
        slot_read = [sem(f"slot_read{s}") for s in range(2)]
        small_done = sem("small_done")
        small_read = sem("small_read")
        ssq_cleared = sem("ssq_cleared")
        squared = sem("squared")
        ssq_added = sem("ssq_added")
        norm_summed = sem("norm_summed")
        norm_part = sem("norm_part")
        mean_ready = sem("mean_ready")
        norm_power = sem("norm_power")
        diag_ready = sem("diag_ready")
        rstd_spread = sem("rstd_spread")
        rstd_copied = sem("rstd_copied")
        normed = sem("normed")
        xg_hi_ready = sem("xg_hi_ready")
        xg_ready = sem("xg_ready")
        xg_read = sem("xg_read")
        h_hi_ready = sem("h_hi_ready")
        h_ready = sem("h_ready")
        x_stored = [sem(f"x_stored{g}") for g in range(4)]
        x_loaded = [sem(f"x_loaded{g}") for g in range(4)]
        rope_loaded = sem("rope_loaded")
        head_loaded = sem("head_loaded")
        state_loaded = sem("state_loaded")
        states_stored = sem("states_stored")
        swapped = sem("swapped")
        swapped_sin = sem("swapped_sin")
        rotated = sem("rotated")
        roped = sem("roped")
        k_hi_ready = sem("k_hi_ready")
        v_hi_ready = sem("v_hi_ready")
        pr_hi_ready = sem("pr_hi_ready")
        pr_split = sem("pr_split")
        z_gate = sem("z_gate")
        scanned = sem("scanned")
        sample_state = sem("sample_state")
        o_squared = sem("o_squared")
        o_mean = sem("o_mean")
        o_power = sem("o_power")
        o_rstd = sem("o_rstd")
        sample_copied = sem("sample_copied")
        o_hi_ready = sem("o_hi_ready")
        o_split = sem("o_split")
        r_cleared = sem("r_cleared")
        r_gated = sem("r_gated")
        conv_kept = sem("conv_kept")
        conv_stored = sem("conv_stored")
        u_ready = sem("u_ready")
        conv_first = sem("conv_first")
        conv_second = sem("conv_second")
        conv_third = sem("conv_third")
        a_gate = sem("a_gate")
        a_product = sem("a_product")
        a_hi_ready = sem("a_hi_ready")
        a_split = sem("a_split")
        merged = sem("merged")
        m_hi_ready = sem("m_hi_ready")
        m_split = sem("m_split")
        y_turned = sem("y_turned")
        y_read = sem("y_read")
        y_scaled = sem("y_scaled")
        y_gained = sem("y_gained")
        y_stored = sem("y_stored")
        g_loaded = sem("g_loaded")

        block = ctx.enter_context(nc.Block())

        def chunk_cols(c):
            return (c * CHUNK, CHUNK) if c < NCH else (SAMP, DEC)

        def head_bases(l, h):
            if isinstance(h, int) and h == 0:
                return l * WL, l * (UL // 2), l * BL
            return l * WL + h * 8 - 2, l * (UL // 2) + h * 7 - 4, l * BL + h * 13 - 3

        B_KT, B_SC, B_V0, B_V1, B_X, B_KVA, B_KVB, B_S, B_OA, B_OB = range(10)

        @block.sync
        def _(sp):
            sp.sem_inc(conv_stored, OPEN)
            sp.dma_start(ident[:, :], ident_c).then_inc(ident_loaded, 16)
            for c in range(NCH):
                sp.dma_start(x_rows[:, c, :], x_prompt[0, c * P:(c + 1) * P, :]).then_inc(rows_loaded[c], 16)
            sp.dma_start(T0[0:DEC, 0:D], x_sample[0]).then_inc(rows_loaded[NCH], 16)

            def load(n, s, src, shape_k, first=False):
                if not first:
                    sp.wait_ge(weights_split, n - 1)
                sp.dma_start(w_raw[s][:, :].rearrange("p (k n) -> p k n", k=shape_k), src).then_inc(weights_loaded[s], 16)

            def w_in_at(l, col):
                return w_in[l, :, ds(col, P)].rearrange("(k p) n -> p k n", p=P)

            def w_r_at(l, h, half):
                return w_r[l, ds(h * DV, DV), half * 512:half * 512 + 512].rearrange("(k p) n -> p k n", p=P)

            def loads_head(l, h, j0=0):
                wb, _, _ = head_bases(l, h)
                order = [K_ + h * DK, Q_ + h * DK, V_ + h * DV, V_ + h * DV + P, ZR + h * DV, ZR + h * DV + P]
                first = isinstance(h, int)
                if not first:
                    order[2:2] = [None, None]
                for j, col in enumerate(order):
                    if j < j0:
                        continue
                    load(wb + j, j % 2, w_r_at(l, h - 1, j - 2) if col is None else w_in_at(l, col), 2 if col is None else KT)

            for j, col in enumerate((K_, Q_)):
                load(j, j, w_in_at(0, col), KT, first=True)
            sp.dma_start(rope[:, :, :], rope_c.rearrange("a p n -> p a n")).then_inc(rope_loaded, 16)
            for l in range(LAYERS):
                if l == 0:
                    sp.wait_ge(x_cols_act, 4)
                    sp.wait_ge(x_cols_dve, 5)
                    for g in range(4):
                        sp.dma_start(x_keep[:, 2 * g:2 * g + 2, :], x[:, 2 * g:2 * g + 2, :]).then_inc(x_stored[g], 16)
                loads_head(l, 0, j0=2)
                with sp.Fori(1, HEADS) as h:
                    loads_head(l, h)
                for j in range(2):
                    load(l * WL + W_GR - 2 + j, j, w_in_at(l, GR + j * P), KT)
                for half in range(2):
                    load(l * WL + W_GR + half, half, w_r_at(l, HEADS - 1, half), 2)
                with sp.Fori(1, KT // 2) as i:
                    for j in range(2):
                        load(l * WL + W_GR + i * 2 + j, j, w_in_at(l, GR + i * (2 * P) + j * P), KT)
                with sp.Fori(0, KT) as m:
                    for j, part in enumerate((HC, C_, B_, ZA)):
                        load(l * WL + W_A + m * 4 + j, j % 2, w_in_at(l, part + m * P), KT)
                with sp.Fori(0, KT) as m:
                    sp.wait_ge(weights_split, l * WL + W_AG + m * 2)
                    load(0, 0, w_in_at(l, GA + m * P), KT, first=True)
                    load(0, 1, w_a[l, :, ds(m * P, P)].rearrange("(k p) n -> p k n", p=P), KT, first=True)
                for j in range(2):
                    load(l * WL + W_O + j, j, w_o[l, :, j * P:(j + 1) * P].rearrange("(k p) n -> p k n", p=P), KT)
                sp.wait_ge(unit_done, l * UL + U_O + OPEN)
                for g in range(4):
                    if g == 2:
                        for j in range(2):
                            load(l * WL + W_O + 2 + j, j, w_o[l, :, (2 + j) * P:(3 + j) * P].rearrange("(k p) n -> p k n", p=P), KT)
                    sp.dma_start(x[:, 2 * g:2 * g + 2, :], x_keep[:, 2 * g:2 * g + 2, :]).then_inc(x_loaded[g], 16)
                if l < LAYERS - 1:
                    sp.dma_start(rope[:, :, :], rope_c.rearrange("a p n -> p a n")).then_inc(rope_loaded, 16)
                else:
                    sp.dma_start(g_rows[:, :], final_g.rearrange("(a n) -> a n", a=1).to_broadcast([P, D])).then_inc(g_loaded, 16)
                sp.wait_ge(conv_kept, KT * (l + 1))
                with nc.allow_non_contiguous_dma(reason="two rows of 1024 from feature-major columns"):
                    for row in range(2):
                        sp.dma_start(conv_p[l, 0, row].rearrange("(k p) -> p k", p=P), conv_keep[:, 0, row, :]).then_inc(conv_stored, 16)
                        sp.dma_start(conv_s[l, 0, row].rearrange("(k p) -> p k", p=P), conv_keep[:, 1, row, :]).then_inc(conv_stored, 16)
                with sp.Fori(2, KT // 2) as i:
                    for j in range(2):
                        load(l * WL + W_O + i * 2 + j, j, w_o[l, :, ds(i * (2 * P) + j * P, P)].rearrange("(k p) n -> p k n", p=P), KT)
                if l < LAYERS - 1:
                    for j, col in enumerate((K_, Q_)):
                        load((l + 1) * WL + j, j, w_in_at(l + 1, col), KT)
                    for g in range(4):
                        sp.wait_ge(slot_read[0], l * (UL // 2) + U_O // 2 + g + 1 + OPEN)
                        sp.wait_ge(slot_read[1], l * (UL // 2) + U_O // 2 + g + 1 + OPEN)
                        sp.dma_start(x_keep[:, 2 * g:2 * g + 2, :], x[:, 2 * g:2 * g + 2, :]).then_inc(x_stored[g], 16)
            for c in (0, 1, 3, 4, 2, 6, 7, 5, 8):
                if c in Y_POOL:
                    sp.wait_ge(y_gained, Y_POOL.index(c) + 1)
                else:
                    sp.wait_ge(y_read, Y_DVE.index(c) + 1)
                if c < NCH:
                    sp.dma_start(y_prompt[0, c * P:(c + 1) * P, :], y_rows[:, c, :]).then_inc(y_stored, 16)
                else:
                    sp.dma_start(y_sample[0], y_rows[0:DEC, c, :]).then_inc(y_stored, 16)
            sp.wait_ge(y_stored, 16 * (NCH + 1))
            sp.wait_ge(conv_stored, 64 * LAYERS + OPEN)
            sp.wait_ge(states_stored, 32 * HEADS * LAYERS + OPEN)

        @block.gpsimd
        def _(pool):
            nc.gpsimd.memset(ones[:, :], 1.0).then_inc(ones_set, 1)
            nc.gpsimd.memset(neg_half[:, :], -0.5).then_inc(ones_set, 1)
            nc.gpsimd.memset(zero[:, :], 0.0).then_inc(ones_set, 1)
            pool.wait_ge(ones_set, 3)

            def split(n, n2, s):
                pool.wait_ge(weights_loaded[s], n2 * 16 + 16)
                pool.wait_ge(weights_started, n + OPEN)
                nc.gpsimd.tensor_tensor(w_hi[s][:, :], w_raw[s][:, :], zero[:, 0:1].to_broadcast([P, D]), ALU.add).then_inc(weights_hi, 1)
                pool.wait_ge(weights_hi, n + 1)
                nc.gpsimd.tensor_tensor(w_lo[s][:, :], w_raw[s][:, :], w_hi[s][:, :].bitcast(F32),
                                        ALU.subtract).then_inc(weights_split, 1)

            def norm_rstd(k):
                pool.wait_ge(mean_ready, k + 1)
                nc.gpsimd.tensor_tensor(power[:, :], means[:, :], neg_half[:, :], ALU.pow).then_inc(norm_power, 1)

            def o_pow(i, rows, c0, n):
                pool.wait_ge(o_mean, i + 1)
                nc.gpsimd.tensor_tensor(power[0:rows, c0:c0 + n], means[0:rows, c0:c0 + n],
                                        neg_half[0:rows, c0:c0 + n], ALU.pow).then_inc(o_power, 1)

            def head(l, h):
                wb, _, _ = head_bases(l, h)
                w2 = l * (WL // 2) + (0 if isinstance(h, int) else h * 4 - 1)
                first = isinstance(h, int)
                n3 = (l * HEADS + h) * 3
                for j in range(2 if first else 1, 6 if first else 8):
                    split(wb + j, w2 + j // 2, j % 2)
                    if first and j == 2:
                        pool.wait_ge(xg_ready, l * KT + KT)
                        nc.gpsimd.tensor_tensor(r[:, 0, :], zero[:, 0:1].to_broadcast([P, COLS]),
                                                zero[:, 0:1].to_broadcast([P, COLS]), ALU.add).then_inc(r_cleared, 1)
                        nc.gpsimd.memset(r[:, 1:KT // 2, :], 0.0).then_inc(r_cleared, 1)
                    elif first and j == 3:
                        nc.gpsimd.memset(r[:, KT // 2:KT, :], 0.0).then_inc(r_cleared, 1)
                last = 6 if first else 8
                split(wb + last, w2 + last // 2, 0)
                o_pow(n3, DEC, 8, 1)
                o_pow(n3 + 1, P, 0, 4)
                o_pow(n3 + 2, P, 4, 4)

            with pool.Fori(0, LAYERS) as l:
                split(l * WL, l * (WL // 2), 0)
                norm_rstd(l)
                split(l * WL + 1, l * (WL // 2), 1)
                head(l, 0)
                with pool.Fori(1, HEADS) as h:
                    head(l, h)
                split(l * WL + W_GR - 1, l * (WL // 2) + W_GR // 2 - 1, 1)
                with pool.Fori(W_GR // 2, WL // 2) as i:
                    for j in range(2):
                        split(l * WL + i * 2 + j, l * (WL // 2) + i, j)
            norm_rstd(LAYERS)
            pool.wait_ge(g_loaded, 16)
            for i, c in enumerate(Y_POOL):
                pool.wait_ge(y_scaled, i + 1)
                nc.gpsimd.tensor_tensor(y_rows[:, c, :], y_rows[:, c, :], g_rows[:, :], ALU.mult).then_inc(y_gained, 1)

        @block.scalar
        def _(act):
            act.sem_inc(states_stored, OPEN)
            act.dma_start(par_rows[PG:PG + 16, :], norm_g.rearrange("l (k p) -> (l k) p", p=P)).then_inc(consts_loaded, 16)
            act.dma_start(par_rows[PW:PW + 48, :], conv_w.rearrange("l w (k p) -> (l w k) p", p=P)).then_inc(consts_loaded, 16)
            act.dma_start(par_rows[PS:PS + 32, :], state_conv.rearrange("l b r (k p) -> (l b r k) p", p=P)).then_inc(consts_loaded, 16)
            act.wait_ge(ones_set, 3)
            nc.scalar.activation(junk[3][:, 0:1], zero[:, :], ACT.Sigmoid).then_inc(act_table, 1)
            for c in range(NCH + 1):
                act.wait_ge(rows_loaded[c], 16)
                _, n = chunk_cols(c)
                src = x_rows[:, c, :] if c < NCH else T0[0:DEC, 0:D]
                nc.scalar.activation(row_squares[0:n, c, :], src, ACT.Square, accum_out=sums[0:n, c:c + 1]).then_inc(rows_squared, 1)
                if c % 2 == 0 and c < NCH:
                    act.wait_ge(rows_turned, c + 1)
                    a, n = chunk_cols(c)
                    nc.scalar.activation(x[:, :, a:a + n], psf[:, 0:KT * n].rearrange("p (k n) -> p k n", k=KT),
                                         ACT.Copy).then_inc(x_cols_act, 1)
            act.wait_ge(x_cols_act, 4)
            act.wait_ge(x_cols_dve, 5)
            act.wait_ge(rows_squared, NCH + 1)
            act.wait_ge(params_turned, 1)
            nc.scalar.activation(par[:, :], ps[:, 6, 0:NPAR], ACT.Copy).then_inc(params_ready, 1)
            act.wait_ge(params_ready, 1)

            def square(l, m):
                act.wait_ge(ssq_added, l * KT + m + OPEN)
                nc.scalar.activation(T0[:, :], x[:, ds(m, 1), :].rearrange("p a n -> p (a n)"), ACT.Square).then_inc(squared, 1)

            def copy_rstd(k):
                act.wait_ge(rstd_spread, k * 2 + 1)
                nc.scalar.activation(rstd_row[:, 0:SEQ], small, ACT.Copy).then_inc(rstd_copied, 1)
                act.wait_ge(rstd_spread, k * 2 + 2)
                nc.scalar.activation(rstd_row[:, SEQ:COLS], ps[:, 6, 0:COLS - SEQ], ACT.Copy).then_inc(rstd_copied, 1)

            def output_high(b):
                act.wait_ge(small_read, b + 1 + OPEN)
                nc.scalar.activation(o_hi[:, :, SAMP:TAIL], T1s, ACT.Copy).then_inc(o_hi_ready, 1)
                for v in range(2):
                    act.wait_ge(small_read, b + v + 2 + OPEN)
                    nc.scalar.activation(o_hi[:, v, 0:SEQ], T1[:, 0:SEQ], ACT.Copy).then_inc(o_hi_ready, 1)

            def head(l, h):
                _, u2, bb = head_bases(l, h)
                first = isinstance(h, int)
                n = l * HEADS + h
                b0 = bb if first else bb + 3
                uv = 2 if first else 10

                def unit(j):
                    act.wait_ge(unit_done, u2 * 2 + j + 1 + OPEN)

                def batch(b):
                    act.wait_ge(small_done, b + 1)

                def swap(j, scale):
                    unit(j)
                    turn = T1 if first and j else T0[:, :]
                    if not (first and j):
                        act.wait_ge(roped, n * 2 + j + OPEN)
                    nc.scalar.activation(cols(turn[0:64, :]), slot(j)[64:128], ACT.Copy, scale=scale).then_inc(swapped, 1)

                act.wait_ge(small_read, bb + OPEN)
                act.dma_start(hc[:, :], head_c[ds(h, 1)].rearrange("a p n -> (a p) n")).then_inc(head_loaded, 16)
                if first:
                    copy_rstd(l)
                    swap(0, DK ** -0.5)
                    for m in range(KT):
                        act.wait_ge(normed, l * KT + m + 1)
                        if m < KT - 1:
                            act.wait_ge(xg_read, l * (KT - 1) + m + 1)
                        else:
                            unit(1)
                        nc.scalar.activation(act_hi[:, m, :], x[:, m, :], ACT.Copy).then_inc(h_hi_ready, 1)
                    act.wait_ge(h_ready, l * KT + KT)
                act.wait_ge(states_stored, n * 32 + OPEN)
                act.dma_start(S[:, NCH + 1, :], state_ret[ds(l, 1), 0, ds(h, 1)].rearrange("a b p n -> (a b p) n")).then_inc(state_loaded, 16)

                if not first:
                    output_high(bb)
                    swap(0, DK ** -0.5)
                swap(1, 1.0)
                batch(b0 + B_KT)
                act.wait_ge(head_loaded, n * 16 + 16)
                nc.scalar.activation(K_hi[:, :, :], small_k, ACT.Identity, scale=hc[:, KDEC:KDEC + 1]).then_inc(k_hi_ready, 1)

                def scores_high():
                    act.wait_ge(small_read, b0 + B_SC + 1 + OPEN)
                    nc.scalar.activation(Pr_hi[:, :, :], T1[:, 0:SEQ].rearrange("p (c n) -> p c n", c=NCH), ACT.Copy).then_inc(pr_hi_ready, 1)

                if not first:
                    scores_high()
                for v, t in enumerate((T0[:, :], T1)):
                    unit(uv + v)
                    if v == 0:
                        act.wait_ge(roped, n * 2 + 2 + OPEN)
                    else:
                        act.wait_ge(pr_split, n + 1)
                    nc.scalar.activation(cols(t), slot(v), ACT.Copy).then_inc(slot_read[v], 1)
                    if first and v == 0:
                        scores_high()
                    batch(b0 + B_V0 + v)
                    nc.scalar.activation(V_hi[:, :, v * P:(v + 1) * P], small_k, ACT.Copy).then_inc(v_hi_ready, 1)
                batch(b0 + B_X)
                nc.scalar.activation(K[0:DEC, NCH, :], k_s, ACT.Identity, scale=hc[0:DEC, KDECS:KDECS + 1])
                nc.scalar.activation(V[0:DEC, NCH, :], v_s, ACT.Copy).then_inc(sample_copied, 1)
                unit(uv + 2)
                nc.scalar.activation(cols(zs[:, 0, :]), slot(0), ACT.Sigmoid).then_inc(z_gate, 1)
                batch(b0 + B_S)
                nc.scalar.activation(junk[0][0:DEC, :], small_v[0:DEC, 2, :], ACT.Square, accum_out=sums[0:DEC, 8:9]).then_inc(o_squared, 1)
                for g in range(2):
                    batch(b0 + B_OA + g)
                    for c in range(4):
                        i = nc.scalar.activation(junk[c][:, :], small_v[:, c, :], ACT.Square, accum_out=sums[:, 4 * g + c:4 * g + c + 1])
                    i.then_inc(o_squared, 1)
                    if g == 0:
                        unit(uv + 3)
                        nc.scalar.activation(cols(zs[:, 1, :]), slot(1), ACT.Sigmoid).then_inc(z_gate, 1)
                act.wait_ge(sample_state, n + 1)
                act.dma_start(ret_p[ds(l, 1), 0, ds(h, 1)].rearrange("a b p n -> (a b p) n"), S[:, NCH - 1, :]).then_inc(states_stored, 16)
                act.dma_start(ret_s[ds(l, 1), 0, ds(h, 1)].rearrange("a b p n -> (a b p) n"), S[:, NCH, :]).then_inc(states_stored, 16)

            with act.Fori(0, LAYERS) as l:
                act.wait_ge(unit_done, l * UL + OPEN)
                for m in range(KT):
                    act.wait_ge(slot_read[m % 2], l * (UL // 2) + OPEN)
                    nc.scalar.activation(act_hi[:, m, :], x[:, m, :], ACT.Copy,
                                         scale=par[:, ds(l * KT + m + PG, 1)]).then_inc(xg_hi_ready, 1)
                head(l, 0)
                with act.Fori(1, HEADS) as h:
                    head(l, h)
                output_high(l * BL + BL - 3)
                for j in range(2):
                    act.wait_ge(unit_done, l * UL + U_GR - 8 + j + 1 + OPEN)
                    act.wait_ge(o_split, (l * HEADS + HEADS) * 3 + OPEN)
                    nc.scalar.activation(cols((T0[:, :], T1)[j]), slot(j), ACT.Sigmoid).then_inc(slot_read[j], 1)
                with act.Fori(1, KT // 2) as i:
                    for j in range(2):
                        act.wait_ge(unit_done, l * UL + U_GR + i * 2 + j + 1 + OPEN)
                        act.wait_ge(r_gated, l * KT + i * 2 + j + OPEN)
                        nc.scalar.activation(cols((T0[:, :], T1)[j]), slot(j), ACT.Sigmoid).then_inc(slot_read[j], 1)
                act.wait_ge(r_gated, l * KT + KT + OPEN)
                act.wait_ge(states_stored, (l + 1) * (32 * HEADS) + OPEN)
                with act.Fori(0, KT) as m:
                    t = l * KT + m
                    u2 = l * (UL // 2) + U_A // 2 + m * 2
                    act.wait_ge(unit_done, u2 * 2 + 1 + OPEN)
                    act.wait_ge(a_split, t + OPEN)
                    nc.scalar.activation(cols(T0[:, :]), slot(0), ACT.Copy).then_inc(slot_read[0], 1)
                    act.wait_ge(u_ready, t + 1)
                    own = par[:, ds(l * 24 + m + (PW + 16), 1)]
                    nc.scalar.activation(T0[:, 0:SEQ], T1[:, 0:SEQ], ACT.Identity, scale=own)
                    nc.scalar.activation(T0[:, SAMP:TAIL], T1[:, U_SAMP:U_SAMP + DEC], ACT.Identity, scale=own).then_inc(conv_first, 1)
                    act.wait_ge(unit_done, u2 * 2 + 4 + OPEN)
                    act.wait_ge(conv_third, t + 1)
                    nc.scalar.activation(cols(T1), slot(1), ACT.Sigmoid).then_inc(a_gate, 1)
                    act.wait_ge(a_product, t + 1)
                    nc.scalar.activation(prod_hi[:, ds(m, 1), :].rearrange("p a n -> p (a n)"), T0[:, :], ACT.Copy).then_inc(a_hi_ready, 1)
                act.wait_ge(a_split, l * KT + KT + OPEN)

                def gate_a(l, m):
                    act.wait_ge(unit_done, l * UL + U_AG + m * 2 + 1 + OPEN)
                    act.wait_ge(merged, l * KT + m + OPEN)
                    nc.scalar.activation(cols(T0[:, :]), slot(0), ACT.Sigmoid).then_inc(slot_read[0], 1)

                with act.Fori(0, KT - 1) as m:
                    gate_a(l, m)
                gate_a(l, KT - 1)
                for m in range(KT):
                    act.wait_ge(merged, l * KT + m + 1 + OPEN)
                    nc.scalar.activation(act_hi[:, m, :], r[:, m, :], ACT.Copy).then_inc(m_hi_ready, 1)
                with act.Fori(0, KT // 2 - 1) as i:
                    for j in range(2):
                        act.wait_ge(slot_read[j], l * (UL // 2) + U_O // 2 + i + 1 + OPEN)
                        square(l, i * 2 + j)
                act.wait_ge(slot_read[0], l * (UL // 2) + UL // 2 + OPEN)
                square(l, KT - 2)
            act.wait_ge(norm_power, LAYERS + 1)
            for c in Y_POOL:
                act.wait_ge(y_turned, c + 1)
                a = 2 * BANK * (c % 3)
                nc.scalar.activation(y_rows[:, c, :], psf[:, a:a + D], ACT.Copy, scale=power[:, c:c + 1]).then_inc(y_scaled, 1)

        @block.vector
        def _(dve):
            V_ = nc.vector
            for free in (small_read, slot_read[0], slot_read[1], roped, ssq_added, r_gated, a_split, merged, o_split):
                dve.sem_inc(free, OPEN)
            V_.memset(x[:, :, TAIL:COLS], 0.0).then_inc(unused_zeroed, 1)
            for s in range(2):
                V_.memset(ps[:, 3 * s + 2, LAST:THIRD], 0.0).then_inc(unused_zeroed, 1)
            V_.memset(means[:, :], 1.0).then_inc(unused_zeroed, 1)
            for c in (1, 3, 5, 7, NCH):
                dve.wait_ge(rows_turned, c + 1)
                a, n = chunk_cols(c)
                o = 3 * BANK * (c % 2)
                V_.tensor_copy(x[:, :, a:a + n], psf[:, o:o + KT * n].rearrange("p (k n) -> p k n", k=KT)).then_inc(x_cols_dve, 1)
            dve.wait_ge(rows_squared, NCH + 1)
            V_.tensor_scalar(means[:, 0:NCH], sums[:, 0:NCH], 1.0 / D, EPS, ALU.mult, ALU.add)
            V_.tensor_scalar(means[0:DEC, 8:9], sums[0:DEC, 8:9], 1.0 / D, EPS, ALU.mult, ALU.add).then_inc(mean_ready, 1)
            dve.wait_ge(params_ready, 1)
            V_.memset(U[:, 0:2], 0.0).then_inc(u_cleared, 1)
            dve.wait_ge(rows_turned, NCH + 1)
            dve.wait_ge(unused_zeroed, 4)

            def add_squares(l, m):
                dve.wait_ge(squared, l * (KT - 1) + m + 1)
                dve.wait_ge(ssq_added, l * KT + m + OPEN)
                V_.tensor_tensor(T1, T1, T0[:, :], ALU.add).then_inc(ssq_added, 1)

            def norm_means(l):
                dve.wait_ge(norm_summed, l + 1)
                V_.tensor_scalar(means[:, 0:NCH], ps[:, 6, 0:NCH], 1.0 / D, EPS, ALU.mult, ALU.add)
                V_.tensor_scalar(means[0:DEC, 8:9], ps[0:DEC, 6, 8:9], 1.0 / D, EPS, ALU.mult, ALU.add).then_inc(norm_part, 1)
                dve.wait_ge(norm_part, l + 1)
                V_.scalar_tensor_tensor(means[:, 0:NCH], ps[:, 6, 16:16 + NCH], 1.0 / D, means[:, 0:NCH], ALU.mult, ALU.add)
                V_.scalar_tensor_tensor(means[0:DEC, 8:9], ps[0:DEC, 6, 24:25], 1.0 / D, means[0:DEC, 8:9], ALU.mult, ALU.add).then_inc(mean_ready, 1)

            def norm_scale(l):
                dve.wait_ge(norm_power, l + 1)
                V_.tensor_tensor(T0[:, 0:SEQ].rearrange("p (c n) -> p c n", n=P), I[:, None, :].to_broadcast([P, NCH, P]),
                                 power[:, 0:NCH, None].to_broadcast([P, NCH, P]), ALU.mult)
                V_.tensor_scalar(T0[0:DEC, SAMP:COLS], I[0:DEC, 0:DEC + 4], power[0:DEC, 8:9], None, ALU.mult).then_inc(diag_ready, 1)

            def gated_output(hn, b):
                dve.wait_ge(small_done, b + 1)
                V_.tensor_tensor(T1s, o_s, zs[:, :, SAMP:TAIL], ALU.mult).then_inc(small_read, 1)
                dve.wait_ge(o_hi_ready, hn * 3 + 1)
                V_.tensor_tensor(o_lo[:, :, SAMP:TAIL], T1s, o_hi[:, :, SAMP:TAIL].bitcast(F32), ALU.subtract).then_inc(o_split, 1)
                for v in range(2):
                    dve.wait_ge(small_done, b + v + 2)
                    dve.wait_ge(o_split, hn * 3 + v + 1 + OPEN)
                    V_.tensor_tensor(T1[:, 0:SEQ], small, zs[:, v, 0:SEQ], ALU.mult).then_inc(small_read, 1)
                    dve.wait_ge(o_hi_ready, hn * 3 + v + 2)
                    V_.tensor_tensor(o_lo[:, v, 0:SEQ], T1[:, 0:SEQ], o_hi[:, v, 0:SEQ].bitcast(F32), ALU.subtract).then_inc(o_split, 1)

            def head(l, h):
                _, u2, bb = head_bases(l, h)
                first = isinstance(h, int)
                n = l * HEADS + h
                b0 = bb if first else bb + 3
                uv = 2 if first else 10

                def unit(j):
                    dve.wait_ge(unit_done, u2 * 2 + j + 1 + OPEN)

                def batch(b):
                    dve.wait_ge(small_done, b + 1)

                def add_r(w):
                    unit(2 + w)
                    V_.tensor_tensor(cols(r[:, w, :]), slot(w % 2), cols(r[:, w, :]), ALU.add).then_inc(slot_read[w % 2], 1)

                def turn(j):
                    return T1 if first and j else T0[:, :]

                def rotate(j, out, scale, meanwhile=None):
                    rotate_slot(j, out, scale)
                    rotate_rest(j, out, meanwhile)

                def rotate_slot(j, out, scale):
                    unit(j)
                    if not (first and j):
                        dve.wait_ge(roped, n * 2 + j + OPEN)
                    V_.tensor_scalar(cols(turn(j)[64:128, :]), slot(j)[0:64], scale, None, ALU.mult)
                    dve.wait_ge(swapped, n * 2 + j + 1)
                    V_.scalar_tensor_tensor(cols(out[:, :]), slot(j), scale, cols(rope[:, 0, :]), ALU.mult, ALU.mult).then_inc(slot_read[j], 1)

                def rotate_rest(j, out, meanwhile=None):
                    dve.wait_ge(slot_read[j], u2 + 1 + OPEN)
                    V_.tensor_tensor(turn(j), turn(j), rope[:, 1, :], ALU.mult).then_inc(swapped_sin, 1)
                    if meanwhile is not None:
                        meanwhile()
                    dve.wait_ge(swapped_sin, n * 2 + j + 1)
                    if first:
                        V_.tensor_tensor(out[:, :], out[:, :], turn(j), ALU.add).then_inc(rotated, 1)
                        dve.wait_ge(rotated, l * 2 + j + 1)
                        V_.tensor_tensor(out[:, :], out[:, :], rstd_row[:, :], ALU.mult).then_inc(roped, 1)
                    else:
                        V_.tensor_tensor(out[:, :], out[:, :], turn(j), ALU.add).then_inc(roped, 1)

                def normal_tile(m):
                    dve.wait_ge(x_stored[m // 2], l * 16 + 16)
                    V_.scalar_tensor_tensor(x[:, m, :], x[:, m, :], par[:, ds(l * KT + m + PG, 1)], rstd_row[:, :],
                                            ALU.mult, ALU.mult).then_inc(normed, 1)

                def scan(c, last):
                    if c == 0:
                        i = V_.tensor_copy(S[:, 0, :], small_v[:, 0, :])
                    else:
                        i = V_.scalar_tensor_tensor(S[:, c, :], S[:, c - 1, :], hc[:, G128:G128 + 1], small_v[:, c % 4, :], ALU.mult, ALU.add)
                    i.then_inc(small_read if last else scanned, 1)

                def normalise(k, rows, c0, nch, src):
                    dve.wait_ge(o_squared, n * 3 + k + 1)
                    V_.tensor_scalar(means[0:rows, c0:c0 + nch], sums[0:rows, c0:c0 + nch], hc[0:rows, OA_:OA_ + 1], EPS, ALU.mult, ALU.add).then_inc(o_mean, 1)
                    dve.wait_ge(o_power, n * 3 + k + 1)
                    V_.tensor_scalar(rstds[0:rows, c0:c0 + nch], power[0:rows, c0:c0 + nch], hc[0:rows, OB_:OB_ + 1], None, ALU.mult).then_inc(o_rstd, 1)
                    dve.wait_ge(o_rstd, n * 3 + k + 1)
                    V_.tensor_tensor(V[0:rows, c0:c0 + nch, :], src, rstds[0:rows, c0:c0 + nch, None].to_broadcast([rows, nch, DV]), ALU.mult).then_inc(small_read, 1)

                dve.wait_ge(rope_loaded, l * 16 + 16)
                if not first:
                    dve.wait_ge(slot_read[1], u2 + OPEN)
                    gated_output(n - 1, bb)
                if first:
                    dve.wait_ge(rstd_copied, l * 2 + 2)
                    for m in range(5):
                        normal_tile(m)
                    rotate_slot(0, kT, DK ** -0.5)
                    for m in range(KT):
                        if 1 <= m < 4:
                            normal_tile(4 + m)
                        dve.wait_ge(h_hi_ready, l * KT + m + 1)
                        V_.tensor_tensor(act_lo[:, m, :], x[:, m, :], act_hi[:, m, :].bitcast(F32), ALU.subtract).then_inc(h_ready, 1)
                    rotate_slot(1, qT, 1.0)
                    rotate_rest(0, kT)
                    rotate_rest(1, qT)
                else:
                    rotate(0, kT, DK ** -0.5)
                    rotate(1, qT, 1.0, lambda: add_r(0))
                if first:
                    dve.wait_ge(r_cleared, l * 3 + 3)
                else:
                    for w in range(1, KT):
                        add_r(w)
                batch(b0 + B_KT)
                dve.wait_ge(head_loaded, n * 16 + 16)
                dve.wait_ge(k_hi_ready, n + 1)
                V_.scalar_tensor_tensor(K_lo[:, :, :], small_k, hc[:, KDEC:KDEC + 1], K_hi[:, :, :].bitcast(F32),
                                        ALU.mult, ALU.subtract).then_inc(small_read, 1)
                batch(b0 + B_SC)
                dve.wait_ge(o_split, n * 3 + OPEN)
                dve.wait_ge(roped, n * 2 + 2 + OPEN)
                decayed = T1[:, 0:SEQ].rearrange("p (c n) -> p c n", c=NCH)
                V_.tensor_tensor(decayed, small_k, hc[:, None, MASK:MASK + CHUNK].to_broadcast([P, NCH, CHUNK]), ALU.mult).then_inc(small_read, 1)
                dve.wait_ge(pr_hi_ready, n + 1)
                V_.tensor_tensor(Pr_lo[:, :, :], decayed, Pr_hi[:, :, :].bitcast(F32), ALU.subtract).then_inc(pr_split, 1)
                for v in range(2):
                    batch(b0 + B_V0 + v)
                    dve.wait_ge(v_hi_ready, n * 2 + v + 1)
                    V_.tensor_tensor(V_lo[:, :, v * P:(v + 1) * P], small_k, V_hi[:, :, v * P:(v + 1) * P].bitcast(F32), ALU.subtract).then_inc(small_read, 1)
                batch(b0 + B_X)
                dve.wait_ge(sample_copied, n + 1)
                V_.tensor_tensor(Pr[0:DEC, NCH, 0:DEC], score_s, hc[0:DEC, MASK:MASK + DEC], ALU.mult).then_inc(small_read, 1)

                def silu(v):
                    unit(uv + 2 + v)
                    dve.wait_ge(z_gate, n * 2 + v + 1)
                    V_.tensor_tensor(cols(zs[:, v, :]), slot(v), cols(zs[:, v, :]), ALU.mult).then_inc(slot_read[v], 1)

                batch(b0 + B_KVA)
                for c in range(4):
                    if c:
                        dve.wait_ge(scanned, n * 6 + c)
                    scan(c, c == 3)
                batch(b0 + B_KVB)
                dve.wait_ge(small_read, b0 + B_KVA + 1 + OPEN)
                for c in range(4, 8):
                    if c > 4:
                        dve.wait_ge(scanned, n * 6 + c - 1)
                    scan(c, c == 7)
                batch(b0 + B_S)
                dve.wait_ge(state_loaded, n * 16 + 16)
                V_.scalar_tensor_tensor(S[:, NCH, :], S[:, NCH + 1, :], hc[:, G64:G64 + 1], small_v[:, 0, :], ALU.mult, ALU.add).then_inc(sample_state, 1)
                normalise(0, DEC, 8, 1, small_v[0:DEC, 2:3, :])
                silu(0)
                batch(b0 + B_OA)
                normalise(1, P, 0, 4, small_v)
                silu(1)
                batch(b0 + B_OB)
                normalise(2, P, 4, 4, small_v)

            def tap(w, back):
                for out, u, n in ((0, 2, SEQ), (SAMP, U_SAMP + 2, DEC)):
                    i = V_.scalar_tensor_tensor(T0[:, out:out + n], U[:, u - back:u - back + n], par[:, ds(w, 1)], T0[:, out:out + n],
                                                ALU.mult, ALU.add)
                return i

            with dve.Fori(0, LAYERS) as l:
                for m in range(KT):
                    if m == 1:
                        norm_scale(l)
                    dve.wait_ge(xg_hi_ready, l * KT + m + 1)
                    V_.scalar_tensor_tensor(act_lo[:, m, :], x[:, m, :], par[:, ds(l * KT + m + PG, 1)],
                                            act_hi[:, m, :].bitcast(F32), ALU.mult, ALU.subtract).then_inc(xg_ready, 1)
                head(l, 0)
                with dve.Fori(1, HEADS) as h:
                    head(l, h)
                dve.wait_ge(slot_read[1], l * (UL // 2) + (U_GR - 8) // 2 + OPEN)
                gated_output(l * HEADS + HEADS - 1, l * BL + BL - 3)
                for w in range(KT):
                    dve.wait_ge(unit_done, l * UL + U_GR - 6 + w + 1 + OPEN)
                    V_.tensor_tensor(cols(r[:, w, :]), slot(w % 2), cols(r[:, w, :]), ALU.add).then_inc(slot_read[w % 2], 1)
                for j in range(2):
                    dve.wait_ge(slot_read[j], l * (UL // 2) + (U_GR - 8) // 2 + 5 + OPEN)
                    V_.tensor_tensor(r[:, j, :], r[:, j, :], (T0[:, :], T1)[j], ALU.mult).then_inc(r_gated, 1)
                with dve.Fori(1, KT // 2) as i:
                    for j in range(2):
                        dve.wait_ge(slot_read[j], l * (UL // 2) + U_GR // 2 + i + 1 + OPEN)
                        rm = r[:, ds(i * 2 + j, 1), :].rearrange("p a n -> p (a n)")
                        V_.tensor_tensor(rm, rm, (T0[:, :], T1)[j], ALU.mult).then_inc(r_gated, 1)
                with dve.Fori(0, KT) as m:
                    t = l * KT + m
                    u2 = l * (UL // 2) + U_A // 2 + m * 2
                    dve.wait_ge(unit_done, u2 * 2 + 2 + OPEN)
                    dve.wait_ge(slot_read[0], u2 + 1 + OPEN)
                    V_.tensor_tensor(T1[:, 0:2 * THIRD].rearrange("p (c n) -> p c n", c=2), ps[:, 3:5, 0:THIRD],
                                     T0[:, 0:2 * THIRD].rearrange("p (c n) -> p c n", c=2), ALU.mult)
                    V_.tensor_tensor(T1[:, 2 * THIRD:SEQ], ps[:, 5, 0:SEQ - 2 * THIRD], T0[:, 2 * THIRD:SEQ], ALU.mult)
                    V_.tensor_tensor(T1[:, U_SAMP:U_SAMP + DEC], ps[:, 5, SEQ - 2 * THIRD:LAST], T0[:, SAMP:TAIL], ALU.mult).then_inc(slot_read[1], 1)
                    dve.wait_ge(slot_read[1], u2 + 1 + OPEN)
                    dve.wait_ge(conv_stored, l * 64 + OPEN)
                    V_.tensor_copy(conv_keep[:, 0, :, ds(m, 1)].rearrange("p r a -> p (r a)"), T1[:, SEQ - 2:SEQ])
                    V_.tensor_copy(conv_keep[:, 1, :, ds(m, 1)].rearrange("p r a -> p (r a)"), T1[:, U_SAMP + DEC - 2:U_SAMP + DEC]).then_inc(conv_kept, 1)
                    V_.tensor_copy(T1[:, SEQ:SEQ + 1], par[:, ds(l * 16 + m + PS, 1)])
                    V_.tensor_copy(T1[:, SEQ + 1:SEQ + 2], par[:, ds(l * 16 + m + (PS + 8), 1)]).then_inc(u_ready, 1)
                    dve.wait_ge(conv_first, t + 1)
                    tap(l * 24 + m + (PW + 8), 1).then_inc(conv_second, 1)
                    dve.wait_ge(conv_second, t + 1)
                    tap(l * 24 + m + PW, 2).then_inc(conv_third, 1)
                    dve.wait_ge(unit_done, u2 * 2 + 3 + OPEN)
                    dve.wait_ge(conv_third, t + 1)
                    V_.tensor_tensor(cols(T0[:, :]), slot(0), cols(T0[:, :]), ALU.mult).then_inc(slot_read[0], 1)
                    dve.wait_ge(a_gate, t + 1)
                    dve.wait_ge(slot_read[0], u2 + 2 + OPEN)
                    V_.tensor_tensor(cols(T0[:, :]), slot(1), cols(T0[:, :]), ALU.mult).then_inc(slot_read[1], 1)
                    dve.wait_ge(slot_read[1], u2 + 2 + OPEN)
                    V_.tensor_tensor(T0[:, :], T0[:, :], T1, ALU.mult).then_inc(a_product, 1)
                    dve.wait_ge(a_hi_ready, t + 1)
                    V_.tensor_tensor(prod_lo[:, ds(m, 1), :].rearrange("p a n -> p (a n)"), T0[:, :],
                                     prod_hi[:, ds(m, 1), :].rearrange("p a n -> p (a n)").bitcast(F32), ALU.subtract).then_inc(a_split, 1)

                def merge(l, m, rm):
                    u2 = l * (UL // 2) + U_AG // 2 + m
                    dve.wait_ge(unit_done, u2 * 2 + 2 + OPEN)
                    dve.wait_ge(slot_read[0], u2 + 1 + OPEN)
                    V_.tensor_tensor(cols(T1), slot(1), cols(T0[:, :]), ALU.mult).then_inc(slot_read[1], 1)
                    dve.wait_ge(slot_read[1], u2 + 1 + OPEN)
                    V_.tensor_tensor(rm, rm, T1, ALU.add).then_inc(merged, 1)

                def merged_low(m):
                    dve.wait_ge(m_hi_ready, l * KT + m + 1)
                    V_.tensor_tensor(act_lo[:, m, :], r[:, m, :], act_hi[:, m, :].bitcast(F32), ALU.subtract).then_inc(m_split, 1)

                with dve.Fori(0, KT - 1) as m:
                    merge(l, m, r[:, ds(m, 1), :].rearrange("p a n -> p (a n)"))
                for m in range(KT - 1):
                    merged_low(m)
                merge(l, KT - 1, r[:, KT - 1, :])
                merged_low(KT - 1)
                V_.memset(T1, 0.0).then_inc(ssq_cleared, 1)
                dve.wait_ge(ssq_cleared, l + 1)
                for g in range(4):
                    dve.wait_ge(x_loaded[g], l * 16 + 16)
                    for j in range(2):
                        m = 2 * g + j
                        dve.wait_ge(unit_done, l * UL + U_O + m + 1 + OPEN)
                        V_.tensor_tensor(cols(x[:, m, :]), slot(j), cols(x[:, m, :]), ALU.add).then_inc(slot_read[j], 1)
                        if m < KT - 1:
                            add_squares(l, m)
                dve.wait_ge(slot_read[1], l * (UL // 2) + UL // 2 + OPEN)
                dve.wait_ge(ssq_added, l * KT + KT - 1 + OPEN)
                V_.tensor_tensor(T0[:, :], x[:, KT - 1, :], x[:, KT - 1, :], ALU.mult).then_inc(ssq_added, 1)
                norm_means(l)
            dve.wait_ge(norm_power, LAYERS + 1)
            dve.wait_ge(g_loaded, 16)
            for c in Y_DVE:
                dve.wait_ge(y_turned, c + 1)
                n = P if c < NCH else DEC
                a = 2 * BANK * (c % 3)
                V_.scalar_tensor_tensor(y_rows[0:n, c, :], psf[0:n, a:a + D], power[0:n, c:c + 1], g_rows[0:n, :],
                                        ALU.mult, ALU.mult).then_inc(y_read, 1)

        @block.tensor
        def _(pe):
            mm = nc.tensor.matmul
            pe.sem_inc(weights_started, OPEN)
            pe.sem_inc(unit_done, OPEN)
            pe.wait_ge(ident_loaded, 16)
            for c in range(NCH + 1):
                pe.wait_ge(rows_loaded[c], 16)
                if c >= 2:
                    pe.wait_ge((x_cols_act, x_cols_dve)[c % 2], c // 2)
                _, n = chunk_cols(c)
                src = x_rows[:, c, :] if c < NCH else T0[0:DEC, 0:D]
                for k in range(KT):
                    a = 3 * BANK * (c % 2) + k * n
                    i = nc.tensor.transpose(psf[:, a:a + n], src[:, k * P:(k + 1) * P], I[0:n, 0:n])
                i.then_inc(rows_turned, 1)
            pe.wait_ge(consts_loaded, 48)
            nc.tensor.transpose(ps[:, 6, 0:NPAR], par_rows[0:NPAR, :], I[0:NPAR, 0:NPAR]).then_inc(params_turned, 1)
            pe.wait_ge(ones_set, 1)
            pe.wait_ge(params_ready, 1)

            def norm_sums(l):
                for t, squares in enumerate((T1, T0[:, :])):
                    pe.wait_ge(ssq_added, l * KT + KT - 1 + t + OPEN)
                    for c in range(NCH + 1):
                        a, n = chunk_cols(c)
                        i = mm(ps[0:n, 6, 16 * t + c:16 * t + c + 1], squares[:, a:a + n], ones[:, 0:1], start=True, stop=True)
                i.then_inc(norm_summed, 1)

            def norm_spread(l):
                pe.wait_ge(diag_ready, l + 1)
                for c in range(NCH):
                    i = mm(small_k[:, c, :], ones[:, :], T0[:, c * P:(c + 1) * P], start=True, stop=True)
                i.then_inc(rstd_spread, 1)

            def norm_spread_sample(l):
                pe.wait_ge(rstd_copied, l * 2 + 1)
                mm(ps[:, 6, 0:COLS - SEQ], ones[0:DEC, :], T0[0:DEC, SAMP:COLS], start=True, stop=True).then_inc(rstd_spread, 1)

            def tile_products(s, ws, hi, lo, k, ktiles, a):
                terms = ((w_hi[ws], hi), (w_hi[ws], lo), (w_lo[ws], hi))
                done = []
                for t, (w, b) in enumerate(terms):
                    for c, cn in enumerate((THIRD, THIRD, LAST)):
                        done.append(mm(ps[:, 3 * s + c, 0:cn], w[:, a:a + P], b[:, k, c * THIRD:c * THIRD + cn],
                                       start=(k == 0 and t == 0), stop=(k == ktiles - 1 and t == 2)))
                return done

            def unit(n, u2, s, hi=act_hi, lo=act_lo, between={}, ready=None, read=None):
                pe.wait_ge(weights_split, n + 1)
                pe.wait_ge(slot_read[s], u2 + OPEN)
                for k in range(KT):
                    if k in between:
                        between[k]()
                    if ready is not None:
                        ready(k)
                    done = tile_products(s, s, hi, lo, k, KT, k * P)
                    if k == 0:
                        done[0].then_inc(weights_started, 1)
                    if read is not None and k < KT - 1:
                        done[-1].then_inc(read, 1)
                done[-1].then_inc(unit_done, 1)

            def w_r_unit(n0, u2, w, o_ready):
                if w % 4 == 0:
                    pe.wait_ge(weights_split, n0 + w // 4 + 1)
                if w == 0:
                    pe.wait_ge(o_split, o_ready + OPEN)
                pe.wait_ge(slot_read[w % 2], u2 + w // 2 + OPEN)
                for k in range(2):
                    done = tile_products(w % 2, w // 4, o_hi, o_lo, k, 2, (w % 4) * P + k * 512)
                    if k == 0 and w % 4 == 0:
                        done[0].then_inc(weights_started, 1)
                done[-1].then_inc(unit_done, 1)

            def turn_output_sample(b):
                pe.wait_ge(small_read, b + OPEN)
                for v in range(2):
                    i = mm(o_s[:, v, :], V[0:DEC, NCH, v * P:(v + 1) * P], I[0:DEC, 0:DEC], start=True, stop=True)
                i.then_inc(small_done, 1)

            def turn_output(v, b):
                pe.wait_ge(small_read, b + OPEN)
                for c in range(NCH):
                    i = nc.tensor.transpose(small_k[:, c, :], V[:, c, v * P:(v + 1) * P], I)
                i.then_inc(small_done, 1)

            def output_batches(bb):
                return {4: lambda: turn_output_sample(bb), 5: lambda: turn_output(0, bb + 1),
                        7: lambda: turn_output(1, bb + 2)}

            def head(l, h):
                n0, u2, bb = head_bases(l, h)
                first = isinstance(h, int)
                n = l * HEADS + h
                b0 = bb if first else bb + 3
                n1, u1 = (n0 + 2, u2 + 1) if first else (n0 + 4, u2 + 5)

                def turn_keys():
                    pe.wait_ge(small_read, b0 + B_KT + OPEN)
                    pe.wait_ge(roped, n * 2 + 1 + OPEN)
                    for c in range(NCH):
                        i = nc.tensor.transpose(small_k[:, c, :], kT[:, c * CHUNK:(c + 1) * CHUNK], I)
                    i.then_inc(small_done, 1)

                def scores():
                    pe.wait_ge(small_read, b0 + B_SC + OPEN)
                    pe.wait_ge(roped, n * 2 + 2 + OPEN)
                    for c in range(NCH):
                        a = c * CHUNK
                        i = mm(small_k[:, c, :], kT[:, a:a + CHUNK], qT[:, a:a + CHUNK], start=True, stop=True)
                    i.then_inc(small_done, 1)

                def turn_values(v):
                    pe.wait_ge(small_read, b0 + B_V0 + v + OPEN)
                    pe.wait_ge(slot_read[v], u1 + 1 + OPEN)
                    for c in range(NCH):
                        i = nc.tensor.transpose(small_k[:, c, :], (T0[:, :], T1)[v][:, c * CHUNK:(c + 1) * CHUNK], I)
                    i.then_inc(small_done, 1)

                def sample_batch():
                    pe.wait_ge(small_read, b0 + B_X + OPEN)
                    mm(score_s, kT[:, SAMP:TAIL], qT[:, SAMP:TAIL], start=True, stop=True)
                    nc.tensor.transpose(k_s, kT[:, SAMP:TAIL], I)
                    for v, src in enumerate((T0[:, :], T1)):
                        i = nc.tensor.transpose(v_s[:, v * P:(v + 1) * P], src[:, SAMP:TAIL], I)
                    i.then_inc(small_done, 1)

                def split_product(out, a_hi, a_lo, c, last):
                    mm(out, a_hi[:, c, :], V_hi[:, c, :], start=True, stop=False)
                    mm(out, a_hi[:, c, :], V_lo[:, c, :], start=False, stop=False)
                    return mm(out, a_lo[:, c, :], V_hi[:, c, :], start=False, stop=last)

                def keys_by_values(g):
                    pe.wait_ge(small_read, b0 + B_KVA + g + OPEN)
                    for c in range(4):
                        i = split_product(small_v[:, c, :], K_hi, K_lo, 4 * g + c, True)
                    i.then_inc(small_done, 1)

                def sample_output():
                    pe.wait_ge(small_read, b0 + B_S + OPEN)
                    pe.wait_ge(state_loaded, n * 16 + 16)
                    mm(small_v[:, 0, :], K[0:DEC, NCH, :], V[0:DEC, NCH, :], start=True, stop=True)
                    mm(small_v[0:DEC, 2, :], Pr[0:DEC, NCH, 0:DEC], V[0:DEC, NCH, :], start=True, stop=False)
                    mm(small_v[0:DEC, 2, :], qT[:, SAMP:TAIL], S[:, NCH + 1, :], start=False, stop=True).then_inc(small_done, 1)

                def outputs(g):
                    pe.wait_ge(small_read, b0 + B_OA + g + OPEN)
                    for c in range(4 * g, 4 * g + 4):
                        i = split_product(small_v[:, c % 4, :], Pr_hi, Pr_lo, c, c == 0)
                        if c:
                            i = mm(small_v[:, c % 4, :], qT[:, c * CHUNK:(c + 1) * CHUNK], S[:, c - 1, :], start=False, stop=True)
                    i.then_inc(small_done, 1)

                if first:
                    unit(n0, u2, 0, ready=lambda k: pe.wait_ge(xg_ready, l * KT + k + 1),
                         between={2: lambda: norm_spread(l), 5: lambda: norm_spread_sample(l)})
                    unit(n0 + 1, u2, 1, read=xg_read)
                else:
                    unit(n0, u2, 0, between=output_batches(bb))
                    unit(n0 + 1, u2, 1)
                    for w in range(KT):
                        w_r_unit(n0 + 2, u2 + 1, w, n * 3)
                if first:
                    unit(n1, u1, 0, ready=lambda k: pe.wait_ge(h_ready, l * KT + k + 1))
                    unit(n1 + 1, u1, 1, between={2: turn_keys, 5: scores, 7: lambda: turn_values(0)})
                else:
                    unit(n1, u1, 0, between={2: turn_keys, 6: scores})
                    unit(n1 + 1, u1, 1, between={3: lambda: turn_values(0)})
                unit(n1 + 2, u1 + 1, 0, between={2: lambda: turn_values(1), 4: sample_batch, 6: lambda: keys_by_values(0)})
                unit(n1 + 3, u1 + 1, 1, between={0: lambda: keys_by_values(1), 2: sample_output, 4: lambda: outputs(0)})
                outputs(1)

            with pe.Fori(0, LAYERS) as l:
                head(l, 0)
                with pe.Fori(1, HEADS) as h:
                    head(l, h)
                for j in range(2):
                    unit(l * WL + W_GR - 2 + j, l * (UL // 2) + (U_GR - 8) // 2, j,
                         between=output_batches(l * BL + BL - 3) if j == 0 else {})
                for w in range(KT):
                    w_r_unit(l * WL + W_GR, l * (UL // 2) + (U_GR - 6) // 2, w, (l * HEADS + HEADS) * 3)
                with pe.Fori(1, KT // 2) as i:
                    for j in range(2):
                        unit(l * WL + W_GR + i * 2 + j, l * (UL // 2) + U_GR // 2 + i, j)
                with pe.Fori(0, KT) as m:
                    for j in range(4):
                        unit(l * WL + W_A + m * 4 + j, l * (UL // 2) + U_A // 2 + m * 2 + j // 2, j % 2)
                with pe.Fori(0, KT) as m:
                    unit(l * WL + W_AG + m * 2, l * (UL // 2) + U_AG // 2 + m, 0)
                    pe.wait_ge(a_split, l * KT + KT + OPEN)
                    unit(l * WL + W_AG + m * 2 + 1, l * (UL // 2) + U_AG // 2 + m, 1, prod_hi, prod_lo)
                for j in range(2):
                    unit(l * WL + W_O + j, l * (UL // 2) + U_O // 2, j,
                         ready=(lambda k: pe.wait_ge(m_split, l * KT + k + 1)) if j == 0 else None)
                with pe.Fori(1, KT // 2) as i:
                    for j in range(2):
                        unit(l * WL + W_O + i * 2 + j, l * (UL // 2) + U_O // 2 + i, j)
                norm_sums(l)
            for c in range(NCH + 1):
                if c - 3 in Y_POOL:
                    pe.wait_ge(y_scaled, Y_POOL.index(c - 3) + 1)
                elif c >= 3:
                    pe.wait_ge(y_read, Y_DVE.index(c - 3) + 1)
                a, n = chunk_cols(c)
                for k in range(KT):
                    o = 2 * BANK * (c % 3) + k * P
                    i = nc.tensor.transpose(psf[0:n, o:o + P], x[:, k, a:a + n], I)
                i.then_inc(y_turned, 1)


_INS = ["x_prompt", "x_sample", "state_conv", "state_ret", "norm_g", "w_in", "conv_w", "w_a", "w_r", "w_o", "final_g"]
_OUTS = [(1, SEQ, D), (1, DEC, D), (LAYERS, 1, 2, D), (LAYERS, 1, HEADS, DK, DV),
         (LAYERS, 1, 2, D), (LAYERS, 1, HEADS, DK, DV)]


def shape_constants(np):
    half = DK // 2
    pos = np.zeros(COLS, np.float32)
    pos[0:SEQ] = np.arange(SEQ)
    pos[SAMP:TAIL] = PAST + np.arange(DEC)
    inv = (1.0 / (10000.0 ** (np.arange(half, dtype=np.float32) / half))).astype(np.float32)
    ang = (inv[:, None] * pos[None, :]).astype(np.float32).astype(np.float64)
    rope = np.zeros((2, P, COLS), np.float32)
    rope[0, 0:half] = rope[0, half:] = np.cos(ang)
    rope[1, 0:half] = -np.sin(ang)
    rope[1, half:] = np.sin(ang)
    heads = np.zeros((HEADS, P, NHC), np.float32)
    i = np.arange(CHUNK, dtype=np.float64)
    for h in range(HEADS):
        g = 1.0 - 2.0 ** (-5.0 - h)
        heads[h, :, MASK:MASK + CHUNK] = np.where(i[None, :] >= i[:, None], g ** -(i[:, None] + 1), 0.0)
        heads[h, :, KDEC] = g ** (CHUNK - 1 - i)
        heads[h, 0:DEC, KDECS] = g ** (DEC - 1 - i[0:DEC])
        heads[h, :, OA_] = g ** (2 * (i + 1)) / DV
        heads[h, :, OB_] = g ** (i + 1)
        heads[h, :, G128] = g ** CHUNK
        heads[h, :, G64] = g ** DEC
    return {"rope_c": rope, "head_c": heads, "ident_c": np.eye(P, dtype=np.float32)}


def kernel(**inputs):
    import numpy as _np
    import concourse.bacc as _bacc
    from concourse import mybir as _mybir
    from concourse.bass_utils import run_bass_kernel_spmd as _run

    nc = _bacc.Bacc("TRN2", target_bir_lowering=False, num_devices=1)
    arrays, args = {}, []
    for name in _INS:
        a = _np.ascontiguousarray(inputs[name])
        arrays[f"in_{name}_dram"] = a
        args.append(nc.dram_tensor(f"in_{name}_dram", a.shape, _mybir.dt.from_np(a.dtype), kind="ExternalInput").ap())
    for name, a in shape_constants(_np).items():
        arrays[name] = a
        args.append(nc.dram_tensor(name, a.shape, _mybir.dt.from_np(a.dtype), kind="ExternalInput").ap())
    for i, shape in enumerate(_OUTS):
        args.append(nc.dram_tensor(f"out_{i}_dram", shape, _mybir.dt.float32, kind="ExternalOutput").ap())
    args.append(nc.dram_tensor("x_keep", (P, KT, COLS), _mybir.dt.float32, kind="Internal").ap())
    build(nc, *args)
    r = _run(nc, [arrays], core_ids=[0])
    return tuple(r.results[0][f"out_{i}_dram"] for i in range(len(_OUTS)))
```
